# Optimizing a Trainium2 kernel written in Bass

```python
import math
import jax, jax.numpy as jnp
from jax import lax
import numpy as np

D_MODEL = 1024
BATCH = 1
SEQ = 256
DEPTH = 2

CHUNK = 64
Q_BLOCK = 128
A_HEADS = 8
A_HEAD_DIM = 64
A_WIDTH = A_HEADS * A_HEAD_DIM
IDX_HEADS = 8
IDX_DIM = 64
TOPK_MAX = 256
B_HEADS = 8
B_Q_LORA = 384
B_KV_LORA = 256
B_NOPE = 64
B_ROPE = 32
B_QK = B_NOPE + B_ROPE
B_V = 64
B_WIDTH = B_HEADS * B_V
ROPE_BASE = 10000.0
REL_BUCKETS = 32
REL_MAX_DIST = 128
D_FF = 2816
CONV_W = 3
EPS = 1e-6

IN_SIZES = (A_WIDTH, A_WIDTH, A_WIDTH,
            IDX_HEADS * IDX_DIM, IDX_DIM, IDX_HEADS,
            B_Q_LORA, B_KV_LORA, B_ROPE,
            D_MODEL, D_MODEL)
IN_COLS = 3 * A_WIDTH + IDX_HEADS * IDX_DIM + IDX_DIM + IDX_HEADS + B_Q_LORA + B_KV_LORA + B_ROPE + 2 * D_MODEL


def rms_norm(x, g):
    xf = x.astype(jnp.float32)
    y = xf * lax.rsqrt(jnp.mean(xf * xf, axis=-1, keepdims=True) + EPS)
    return (y * g.astype(jnp.float32)).astype(x.dtype)

def split_cols(z):
    out, start = [], 0
    for n in IN_SIZES:
        out.append(z[..., start:start + n])
        start += n
    return out

def rope(x, pos):
    half = x.shape[-1] // 2
    inv = ROPE_BASE ** (-jnp.arange(half, dtype=jnp.float32) / half)
    ang = pos.astype(jnp.float32)[:, None] * inv[None, :]
    cos = jnp.cos(ang)[:, None, :]
    sin = jnp.sin(ang)[:, None, :]
    xf = x.astype(jnp.float32)
    x1, x2 = xf[..., :half], xf[..., half:]
    return jnp.concatenate([x1 * cos - x2 * sin, x1 * sin + x2 * cos], axis=-1).astype(x.dtype)

def t5_bucket(rel):
    nb = REL_BUCKETS // 2
    max_exact = nb // 2
    side = jnp.where(rel > 0, nb, 0)
    n = jnp.abs(rel)
    nf = jnp.maximum(n, 1).astype(jnp.float32)
    large = max_exact + (jnp.log(nf / max_exact) / math.log(REL_MAX_DIST / max_exact)
                         * (nb - max_exact)).astype(jnp.int32)
    large = jnp.minimum(large, nb - 1)
    return side + jnp.where(n < max_exact, n, large)

def sparse_indexed_attention(q, k, v, q_idx, k_idx, w_idx, rel_bias, topk):
    B, S = q.shape[0], q.shape[1]
    n_blk = S // Q_BLOCK
    key_chunk = jnp.arange(S, dtype=jnp.int32) // CHUNK
    bidx = jnp.arange(B)[:, None, None]
    scale = A_HEAD_DIM ** -0.5
    idx_scale = (IDX_HEADS ** -0.5) * (IDX_DIM ** -0.5)

    def block(i):
        t0 = i * Q_BLOCK
        tq = t0 + jnp.arange(Q_BLOCK, dtype=jnp.int32)
        qi = lax.dynamic_slice_in_dim(q_idx, t0, Q_BLOCK, axis=1)
        wi = lax.dynamic_slice_in_dim(w_idx, t0, Q_BLOCK, axis=1).astype(jnp.float32)
        rel = jax.nn.relu(jnp.einsum('bthd,bsd->bths', qi, k_idx).astype(jnp.float32))
        score = jnp.einsum('bths,bth->bts', rel, wi) * idx_scale
        admissible = key_chunk[None, :] <= (tq // CHUNK)[:, None]
        score = jnp.where(admissible[None], score, -jnp.inf)
        _, sel = lax.top_k(score, topk)
        valid = (sel // CHUNK) <= (tq // CHUNK)[None, :, None]
        k_sel = k[bidx, sel]
        v_sel = v[bidx, sel]
        qb = lax.dynamic_slice_in_dim(q, t0, Q_BLOCK, axis=1)
        logits = jnp.einsum('bthd,btkhd->bthk', qb, k_sel).astype(jnp.float32) * scale
        bias = rel_bias[t5_bucket(sel - tq[None, :, None])]
        logits = logits + jnp.moveaxis(bias, -1, 2).astype(jnp.float32)
        logits = jnp.where(valid[:, :, None, :], logits, -jnp.inf)
        p = jax.nn.softmax(logits, axis=-1).astype(v.dtype)
        return jnp.einsum('bthk,btkhd->bthd', p, v_sel)

    out = lax.map(block, jnp.arange(n_blk))
    return jnp.moveaxis(out, 0, 1).reshape(B, S, A_WIDTH)

def latent_attention(q, k, v):
    B, S = q.shape[0], q.shape[1]
    n_blk = S // Q_BLOCK
    key_chunk = jnp.arange(S, dtype=jnp.int32) // CHUNK
    scale = B_QK ** -0.5

    def block(i):
        t0 = i * Q_BLOCK
        tq = t0 + jnp.arange(Q_BLOCK, dtype=jnp.int32)
        qb = lax.dynamic_slice_in_dim(q, t0, Q_BLOCK, axis=1)
        logits = jnp.einsum('bthd,bshd->bhts', qb, k).astype(jnp.float32) * scale
        mask = key_chunk[None, :] <= (tq // CHUNK)[:, None]
        logits = jnp.where(mask[None, None], logits, -jnp.inf)
        p = jax.nn.softmax(logits, axis=-1).astype(v.dtype)
        return jnp.einsum('bhts,bshd->bthd', p, v)

    out = lax.map(block, jnp.arange(n_blk))
    return jnp.moveaxis(out, 0, 1).reshape(B, S, B_WIDTH)

def causal_dwconv(u, w, b):
    S = u.shape[1]
    up = jnp.pad(u, ((0, 0), (CONV_W - 1, 0), (0, 0)))
    acc = b
    for j in range(CONV_W):
        acc = acc + w[j] * up[:, j:j + S]
    return acc

def first_inputs(seed: int = 0) -> dict:
    key = jax.random.key(seed)
    ks = jax.random.split(key, 22)
    f32 = jnp.float32
    L = DEPTH

    def lin(k, shape, fan_in):
        return jax.random.normal(k, shape, f32) * fan_in ** -0.5

    def gain(k, shape):
        return 1.0 + 0.02 * jax.random.normal(k, shape, f32)

    return {
        "x": jax.random.normal(ks[0], (BATCH, SEQ, D_MODEL), f32),
        "rel_bias": 0.1 * jax.random.normal(ks[1], (REL_BUCKETS, A_HEADS), f32),
        "norm_mix": gain(ks[2], (L, D_MODEL)),
        "w_in": lin(ks[3], (L, D_MODEL, IN_COLS), D_MODEL),
        "a_q_norm": gain(ks[4], (L, A_HEAD_DIM)),
        "a_k_norm": gain(ks[5], (L, A_HEAD_DIM)),
        "b_cq_norm": gain(ks[6], (L, B_Q_LORA)),
        "b_ckv_norm": gain(ks[7], (L, B_KV_LORA)),
        "b_w_uq": lin(ks[8], (L, B_Q_LORA, B_HEADS * B_QK), B_Q_LORA),
        "b_w_ukv": lin(ks[9], (L, B_KV_LORA, B_HEADS * (B_NOPE + B_V)), B_KV_LORA),
        "b_q_norm": gain(ks[10], (L, B_QK)),
        "b_k_norm": gain(ks[11], (L, B_QK)),
        "w_proj_a": lin(ks[12], (L, A_WIDTH, D_MODEL), A_WIDTH),
        "w_proj_b": lin(ks[13], (L, B_WIDTH, D_MODEL), B_WIDTH),
        "b_gate": 0.01 * jax.random.normal(ks[14], (L, 2 * D_MODEL), f32),
        "w_out": lin(ks[15], (L, D_MODEL, D_MODEL), D_MODEL),
        "norm_ffn": gain(ks[16], (L, D_MODEL)),
        "w_up": lin(ks[17], (L, D_MODEL, 2 * D_FF), D_MODEL),
        "conv_w": lin(ks[18], (L, CONV_W, 2 * D_FF), CONV_W),
        "conv_b": 0.01 * jax.random.normal(ks[19], (L, 2 * D_FF), f32),
        "w_down": lin(ks[20], (L, D_FF, D_MODEL), D_FF),
    }

def first_block(x, rel_bias, norm_mix, w_in, a_q_norm, a_k_norm, b_cq_norm, b_ckv_norm,
              b_w_uq, b_w_ukv, b_q_norm, b_k_norm, w_proj_a, w_proj_b, b_gate, w_out,
              norm_ffn, w_up, conv_w, conv_b, w_down):
    B, S, _ = x.shape
    topk = min(TOPK_MAX, S // 4)
    pos = jnp.arange(S, dtype=jnp.int32)
    for l in range(DEPTH):
        h = rms_norm(x, norm_mix[l])
        z = h @ w_in[l]
        qa, ka, va, qi, ki, wi, cq, ckv, kr, ga, gb = split_cols(z)

        qa = rms_norm(qa.reshape(B, S, A_HEADS, A_HEAD_DIM), a_q_norm[l])
        ka = rms_norm(ka.reshape(B, S, A_HEADS, A_HEAD_DIM), a_k_norm[l])
        va = va.reshape(B, S, A_HEADS, A_HEAD_DIM)
        qi = qi.reshape(B, S, IDX_HEADS, IDX_DIM)
        y_a = sparse_indexed_attention(qa, ka, va, qi, ki, wi, rel_bias, topk)

        cq = rms_norm(cq, b_cq_norm[l])
        qb = (cq @ b_w_uq[l]).reshape(B, S, B_HEADS, B_QK)
        qb = jnp.concatenate([qb[..., :B_NOPE], rope(qb[..., B_NOPE:], pos)], axis=-1)
        ckv = rms_norm(ckv, b_ckv_norm[l])
        kv = (ckv @ b_w_ukv[l]).reshape(B, S, B_HEADS, B_NOPE + B_V)
        k_rope = jnp.broadcast_to(rope(kr[:, :, None, :], pos), (B, S, B_HEADS, B_ROPE))
        kb = jnp.concatenate([kv[..., :B_NOPE], k_rope], axis=-1)
        vb = kv[..., B_NOPE:]
        qb = rms_norm(qb, b_q_norm[l])
        kb = rms_norm(kb, b_k_norm[l])
        y_b = latent_attention(qb, kb, vb)

        gate_a = jax.nn.sigmoid(ga + b_gate[l, :D_MODEL])
        gate_b = jax.nn.sigmoid(gb + b_gate[l, D_MODEL:])
        merged = gate_a * (y_a @ w_proj_a[l]) + gate_b * (y_b @ w_proj_b[l])
        x = x + merged @ w_out[l]

        h = rms_norm(x, norm_ffn[l])
        u = causal_dwconv(h @ w_up[l], conv_w[l], conv_b[l])
        val, gat = u[..., :D_FF], u[..., D_FF:]
        x = x + (jax.nn.silu(gat) * val) @ w_down[l]
    return x


DEPTH_2 = 1

CTX_LEN = 256
GRID_W = 64
H_A = 4
DK_A = 128
DV_A = 128
C_A = H_A * DV_A
SHORT_CONV = 5
H_B = 8
N_B = 64
C_B = H_B * N_B
LORA_W = 64
LORA_A = 64
LORA_G = 128
A_COLS = 4 * C_A + 4 * H_A
B_COLS = 3 * C_B + 2 * LORA_W + 2 * LORA_A + LORA_G
IN_COLS_2 = A_COLS + B_COLS + 2 * D_MODEL
N_GROUPS = 4
EXPERTS_PER_GROUP = 8
N_EXPERTS = N_GROUPS * EXPERTS_PER_GROUP
TOP_K = 2
D_EXPERT = 256
NORM_EPS = 1e-6
LNX_EPS = 1e-5 * N_B


def rmsnorm(x, g):
    xf = x.astype(jnp.float32)
    y = xf * lax.rsqrt(jnp.mean(xf * xf, axis=-1, keepdims=True) + NORM_EPS)
    return y.astype(x.dtype) * g

def l2norm(x):
    xf = x.astype(jnp.float32)
    return (xf * lax.rsqrt(jnp.sum(xf * xf, axis=-1, keepdims=True) + NORM_EPS)).astype(x.dtype)

def modulate(x, shift, scale):
    return x * (1 + scale) + shift

def both_dirs(t):
    return jnp.stack([t, jnp.flip(t, 1)], 0)

def per_dir(t):
    return jnp.stack([t[:, :, 0], jnp.flip(t[:, :, 1], 1)], 0)

def merge_dirs(y):
    return y[0] + jnp.flip(y[1], 1)

def to_col_major(x, rows):
    b, l, c = x.shape
    return x.reshape(b, rows, GRID_W, c).transpose(0, 2, 1, 3).reshape(b, l, c)

def to_row_major(x, rows):
    b, l, c = x.shape
    return x.reshape(b, GRID_W, rows, c).transpose(0, 2, 1, 3).reshape(b, l, c)

def depthwise_conv(x, w):
    pad = SHORT_CONV // 2
    return lax.conv_general_dilated(x, w[:, None, :], window_strides=(1,), padding=[(pad, pad)],
                                    dimension_numbers=('NWC', 'WIO', 'NWC'),
                                    feature_group_count=x.shape[-1])

def bidir_shift(x):
    xp = jnp.pad(x, ((0, 0), (1, 1), (0, 0)))
    return 0.5 * (xp[:, :-2] + xp[:, 2:])

def gated_delta_chunked(q, k, v, g, beta, s0):
    dtype = v.dtype
    q, k, v, g, beta = (t.astype(jnp.float32) for t in (q, k, v, g, beta))
    n = q.shape[-2] // CHUNK
    dv = v.shape[-1]

    def blk(t):
        return t.reshape(t.shape[:-2] + (n, CHUNK, t.shape[-1]))

    q, k, v = blk(q), blk(k), blk(v)
    g = g.reshape(g.shape[:-1] + (n, CHUNK))
    beta = beta.reshape(beta.shape[:-1] + (n, CHUNK))
    gc = jnp.cumsum(g, axis=-1)
    incl = jnp.tril(jnp.ones((CHUNK, CHUNK), bool))
    strict = jnp.tril(jnp.ones((CHUNK, CHUNK), bool), -1)
    decay = jnp.where(incl, jnp.exp(jnp.where(incl, gc[..., :, None] - gc[..., None, :], 0.0)), 0.0)
    k_beta = k * beta[..., None]
    lower = jnp.where(strict, jnp.einsum('...id,...jd->...ij', k_beta, k) * decay, 0.0)
    a_mat = jnp.eye(CHUNK, dtype=jnp.float32) + lower
    rhs = jnp.concatenate([v * beta[..., None], k_beta * jnp.exp(gc)[..., None]], axis=-1)
    sol = lax.linalg.triangular_solve(a_mat, rhs, left_side=True, lower=True, unit_diagonal=True)
    u, w = sol[..., :dv], sol[..., dv:]
    qk = jnp.where(incl, jnp.einsum('...id,...jd->...ij', q, k) * decay, 0.0)
    q_dec = q * jnp.exp(gc)[..., None]
    k_dec = k * jnp.exp(gc[..., -1:] - gc)[..., None]
    g_end = jnp.exp(gc[..., -1])
    xs = (jnp.moveaxis(u, -3, 0), jnp.moveaxis(w, -3, 0), jnp.moveaxis(qk, -3, 0),
          jnp.moveaxis(q_dec, -3, 0), jnp.moveaxis(k_dec, -3, 0), jnp.moveaxis(g_end, -1, 0))

    def step(s, inp):
        u_c, w_c, qk_c, qd_c, kd_c, ge_c = inp
        v_new = u_c - jnp.einsum('...ck,...kv->...cv', w_c, s)
        o_c = jnp.einsum('...ck,...kv->...cv', qd_c, s) + jnp.einsum('...ij,...jv->...iv', qk_c, v_new)
        s = s * ge_c[..., None, None] + jnp.einsum('...ck,...cv->...kv', kd_c, v_new)
        return s, o_c

    s_fin, o = lax.scan(step, s0.astype(jnp.float32), xs)
    o = jnp.moveaxis(o, 0, -3)
    return o.reshape(o.shape[:-3] + (n * CHUNK, dv)).astype(dtype), s_fin

def gdn_branch(cols, s0, conv_w, a_log, dt_bias, onorm_g):
    bsz, length, _ = cols.shape
    qkv, z, a, bt = jnp.split(cols, [3 * C_A, 4 * C_A, 4 * C_A + 2 * H_A], axis=-1)
    qkv = jax.nn.silu(depthwise_conv(qkv, conv_w))
    q, k, v = (t.reshape(bsz, length, H_A, DK_A) for t in jnp.split(qkv, 3, axis=-1))
    q = l2norm(q) * DK_A ** -0.5
    k = l2norm(k)
    g = -jnp.exp(a_log) * jax.nn.softplus(a.reshape(bsz, length, 2, H_A) + dt_bias)
    beta = jax.nn.sigmoid(bt.reshape(bsz, length, 2, H_A))
    sw = lambda t: jnp.swapaxes(t, 2, 3)
    o, s_fin = gated_delta_chunked(sw(both_dirs(q)), sw(both_dirs(k)), sw(both_dirs(v)),
                                   sw(per_dir(g)), sw(per_dir(beta)), s0)
    o = merge_dirs(sw(o))
    o = rmsnorm(o, onorm_g) * jax.nn.silu(z.reshape(bsz, length, H_A, DV_A))
    return o.reshape(bsz, length, C_A), s_fin

def rwkv7_scan(r, w, k, v, a, b, s0):
    dtype = r.dtype
    xs = tuple(jnp.moveaxis(t.astype(jnp.float32), 2, 0) for t in (r, w, k, v, a, b))

    def step(s, inp):
        r_t, w_t, k_t, v_t, a_t, b_t = inp
        sa = jnp.einsum('...vk,...k->...v', s, a_t)
        s = s * w_t[..., None, :] + sa[..., :, None] * b_t[..., None, :] + v_t[..., :, None] * k_t[..., None, :]
        return s, jnp.einsum('...vk,...k->...v', s, r_t)

    s_fin, y = lax.scan(step, s0.astype(jnp.float32), xs)
    return jnp.moveaxis(y, 0, 2).astype(dtype), s_fin

def rwkv_branch(cols, s0, mu, w0, w2, a0, a2, g2, k_k, k_a, r_k, lnx_g, lnx_b):
    bsz, length, _ = cols.shape
    cols = cols + (bidir_shift(cols) - cols) * mu
    r, k, v, w_lo, a_lo, g_lo = jnp.split(
        cols, [C_B, 2 * C_B, 3 * C_B, 3 * C_B + 2 * LORA_W, 3 * C_B + 2 * LORA_W + 2 * LORA_A], axis=-1)
    w_lo = w_lo.reshape(bsz, length, 2, LORA_W)
    a_lo = a_lo.reshape(bsz, length, 2, LORA_A)
    w_log = -jax.nn.softplus(-(w0 + jnp.einsum('bldr,drc->bldc', jnp.tanh(w_lo), w2))) - 0.5
    decay = jnp.exp(-jnp.exp(w_log.astype(jnp.float32))).astype(cols.dtype)
    iclr = jax.nn.sigmoid(a0 + jnp.einsum('bldr,drc->bldc', a_lo, a2))
    gate = jax.nn.sigmoid(g_lo) @ g2
    heads = lambda t: t.reshape(t.shape[:-1] + (H_B, N_B))
    kk = l2norm(heads(k * k_k))
    k_dir = heads(k[:, :, None, :] * (1 + (iclr - 1) * k_a))
    b_dir = kk[:, :, None] * heads(iclr)
    r_h, v_h = heads(r), heads(v)
    y, s_fin = rwkv7_scan(both_dirs(r_h), per_dir(heads(decay)), per_dir(k_dir), both_dirs(v_h),
                          both_dirs(-kk), per_dir(b_dir), s0)
    yf = merge_dirs(y).astype(jnp.float32)
    mean = jnp.mean(yf, axis=-1, keepdims=True)
    var = jnp.mean(jnp.square(yf - mean), axis=-1, keepdims=True)
    y = ((yf - mean) * lax.rsqrt(var + LNX_EPS)).astype(cols.dtype).reshape(bsz, length, C_B) * lnx_g + lnx_b
    bonus = jnp.einsum('blhn,bldhn,hn->blh', r_h, k_dir, r_k)[..., None] * v_h
    y = (y + bonus.reshape(bsz, length, C_B)) * gate
    return y, s_fin

def merge_branches(gates, o_a, o_b, w_o_a, w_o_b, w_out):
    g_a, g_b = jnp.split(gates, 2, axis=-1)
    y = jax.nn.sigmoid(g_a) * (o_a @ w_o_a) + jax.nn.sigmoid(g_b) * (o_b @ w_o_b)
    return y @ w_out

def mixing_sublayer(u_lat, u_ctx, rows, with_ctx_out, w_in, gdn_conv, gdn_a_log, gdn_dt_bias, gdn_onorm_g,
                    rwkv_mu, rwkv_w0, rwkv_w2, rwkv_a0, rwkv_a2, rwkv_g2, rwkv_k_k, rwkv_k_a, rwkv_r_k,
                    rwkv_lnx_g, rwkv_lnx_b, w_o_a, w_o_b, w_out):
    bsz = u_lat.shape[0]
    split_at = [A_COLS, A_COLS + B_COLS]
    a_lat, b_lat, gates_lat = jnp.split(u_lat @ w_in, split_at, axis=-1)
    a_ctx, b_ctx, gates_ctx = jnp.split(u_ctx @ w_in, split_at, axis=-1)

    def run_a(cols, s0):
        return gdn_branch(cols, s0, gdn_conv, gdn_a_log, gdn_dt_bias, gdn_onorm_g)

    def run_b(cols, s0):
        return rwkv_branch(cols, s0, rwkv_mu, rwkv_w0, rwkv_w2, rwkv_a0, rwkv_a2, rwkv_g2,
                           rwkv_k_k, rwkv_k_a, rwkv_r_k, rwkv_lnx_g, rwkv_lnx_b)

    zeros_a = jnp.zeros((2, bsz, H_A, DK_A, DV_A), jnp.float32)
    zeros_b = jnp.zeros((2, bsz, H_B, N_B, N_B), jnp.float32)
    oa_ctx, state_a = run_a(a_ctx, zeros_a)
    ob_ctx, state_b = run_b(b_ctx, zeros_b)
    oa_lat, _ = run_a(a_lat, state_a)
    ob_lat, _ = run_b(to_col_major(b_lat, rows), state_b)
    ob_lat = to_row_major(ob_lat, rows)
    y_lat = merge_branches(gates_lat, oa_lat, ob_lat, w_o_a, w_o_b, w_out)
    if not with_ctx_out:
        return y_lat, None
    return y_lat, merge_branches(gates_ctx, oa_ctx, ob_ctx, w_o_a, w_o_b, w_out)

def hier_moe(h, router_grp, router_grp_b, router_exp, router_exp_b, w_gate, w_up, w_down):
    shape = h.shape
    t = h.reshape(-1, shape[-1])
    grp_p = jax.nn.softmax((t @ router_grp + router_grp_b).astype(jnp.float32), axis=-1)
    p_grp, g_sel = lax.top_k(grp_p, 1)
    exp_logits = (t @ router_exp + router_exp_b).astype(jnp.float32).reshape(-1, N_GROUPS, EXPERTS_PER_GROUP)
    in_grp = jnp.take_along_axis(exp_logits, g_sel[:, :, None], axis=1)[:, 0]
    top_logit, top_idx = lax.top_k(in_grp, TOP_K)
    w_top = jax.nn.softmax(top_logit, axis=-1) * p_grp
    w_exp = jnp.einsum('tk,tke->te', w_top, jax.nn.one_hot(top_idx, EXPERTS_PER_GROUP, dtype=jnp.float32))
    combine = (jax.nn.one_hot(g_sel[:, 0], N_GROUPS, dtype=jnp.float32)[:, :, None]
               * w_exp[:, None, :]).astype(h.dtype)
    out = jnp.zeros_like(t)
    for grp in range(N_GROUPS):
        hid = jax.nn.silu(jnp.einsum('td,edf->tef', t, w_gate[grp])) * jnp.einsum('td,edf->tef', t, w_up[grp])
        out = out + jnp.einsum('tef,efd->td', hid * combine[:, grp, :, None], w_down[grp])
    return out.reshape(shape)

def second_inputs(seed: int = 0) -> dict:
    key = jax.random.key(seed)
    ks = jax.random.split(key, 36)
    d = D_MODEL
    nl = DEPTH_2

    def nrm(k, shape, scale):
        return jax.random.normal(k, shape, jnp.float32) * scale

    dt = jnp.exp(jax.random.uniform(ks[11], (nl, 2, H_A), minval=math.log(1e-3), maxval=math.log(1e-1)))
    return {
        'x': nrm(ks[0], (BATCH, SEQ, d), 1.0),
        'c': nrm(ks[1], (BATCH, d), 1.0),
        'ctx': nrm(ks[2], (BATCH, CTX_LEN, d), 1.0),
        'c_ctx': nrm(ks[3], (d,), 1.0),
        'ada_w': nrm(ks[4], (nl, d, 6 * d), 0.5 * d ** -0.5),
        'ada_b': nrm(ks[5], (nl, 6 * d), 0.01),
        'norm_mix_g': 1.0 + nrm(ks[6], (nl, d), 0.05),
        'norm_ffn_g': 1.0 + nrm(ks[7], (nl, d), 0.05),
        'w_in': nrm(ks[8], (nl, d, IN_COLS_2), d ** -0.5),
        'gdn_conv': nrm(ks[9], (nl, SHORT_CONV, 3 * C_A), SHORT_CONV ** -0.5),
        'gdn_a_log': jnp.log(jax.random.uniform(ks[10], (nl, 2, H_A), minval=1.0, maxval=16.0)),
        'gdn_dt_bias': dt + jnp.log(-jnp.expm1(-dt)),
        'gdn_onorm_g': 1.0 + nrm(ks[12], (nl, DV_A), 0.05),
        'rwkv_mu': jax.random.uniform(ks[13], (nl, B_COLS)),
        'rwkv_w0': jax.random.uniform(ks[14], (nl, 2, C_B), minval=-6.0, maxval=-1.0),
        'rwkv_w2': nrm(ks[15], (nl, 2, LORA_W, C_B), 0.1),
        'rwkv_a0': nrm(ks[16], (nl, 2, C_B), 0.1),
        'rwkv_a2': nrm(ks[17], (nl, 2, LORA_A, C_B), 0.1),
        'rwkv_g2': nrm(ks[18], (nl, LORA_G, C_B), LORA_G ** -0.5),
        'rwkv_k_k': 0.85 + nrm(ks[19], (nl, C_B), 0.05),
        'rwkv_k_a': 1.0 + nrm(ks[20], (nl, C_B), 0.05),
        'rwkv_r_k': nrm(ks[21], (nl, H_B, N_B), 0.1),
        'rwkv_lnx_g': 1.0 + nrm(ks[22], (nl, C_B), 0.05),
        'rwkv_lnx_b': nrm(ks[23], (nl, C_B), 0.01),
        'w_o_a': nrm(ks[24], (nl, C_A, d), C_A ** -0.5),
        'w_o_b': nrm(ks[25], (nl, C_B, d), C_B ** -0.5),
        'w_out': nrm(ks[26], (nl, d, d), d ** -0.5),
        'router_grp': nrm(ks[27], (nl, d, N_GROUPS), d ** -0.5),
        'router_grp_b': nrm(ks[28], (nl, N_GROUPS), 0.01),
        'router_exp': nrm(ks[29], (nl, d, N_EXPERTS), d ** -0.5),
        'router_exp_b': nrm(ks[30], (nl, N_EXPERTS), 0.01),
        'moe_w_gate': nrm(ks[31], (nl, N_GROUPS, EXPERTS_PER_GROUP, d, D_EXPERT), d ** -0.5),
        'moe_w_up': nrm(ks[32], (nl, N_GROUPS, EXPERTS_PER_GROUP, d, D_EXPERT), d ** -0.5),
        'moe_w_down': nrm(ks[33], (nl, N_GROUPS, EXPERTS_PER_GROUP, D_EXPERT, d), D_EXPERT ** -0.5),
        'final_norm_g': 1.0 + nrm(ks[34], (d,), 0.05),
    }

def second_block(x, c, ctx, c_ctx, ada_w, ada_b, norm_mix_g, norm_ffn_g, w_in, gdn_conv, gdn_a_log, gdn_dt_bias,
              gdn_onorm_g, rwkv_mu, rwkv_w0, rwkv_w2, rwkv_a0, rwkv_a2, rwkv_g2, rwkv_k_k, rwkv_k_a, rwkv_r_k,
              rwkv_lnx_g, rwkv_lnx_b, w_o_a, w_o_b, w_out, router_grp, router_grp_b, router_exp, router_exp_b,
              moe_w_gate, moe_w_up, moe_w_down, final_norm_g):
    rows = x.shape[1] // GRID_W
    s_lat = jax.nn.silu(c)[:, None, :]
    s_ctx = jax.nn.silu(c_ctx)
    h_lat, h_ctx = x, ctx
    for l in range(DEPTH_2):
        last = l == DEPTH_2 - 1
        m_lat = jnp.split(s_lat @ ada_w[l] + ada_b[l], 6, axis=-1)
        m_ctx = jnp.split(s_ctx @ ada_w[l] + ada_b[l], 6, axis=-1)
        u_lat = modulate(rmsnorm(h_lat, norm_mix_g[l]), m_lat[0], m_lat[1])
        u_ctx = modulate(rmsnorm(h_ctx, norm_mix_g[l]), m_ctx[0], m_ctx[1])
        y_lat, y_ctx = mixing_sublayer(
            u_lat, u_ctx, rows, not last, w_in[l], gdn_conv[l], gdn_a_log[l], gdn_dt_bias[l], gdn_onorm_g[l],
            rwkv_mu[l], rwkv_w0[l], rwkv_w2[l], rwkv_a0[l], rwkv_a2[l], rwkv_g2[l], rwkv_k_k[l], rwkv_k_a[l],
            rwkv_r_k[l], rwkv_lnx_g[l], rwkv_lnx_b[l], w_o_a[l], w_o_b[l], w_out[l])
        h_lat = h_lat + m_lat[2] * y_lat
        h_lat = h_lat + m_lat[5] * hier_moe(
            modulate(rmsnorm(h_lat, norm_ffn_g[l]), m_lat[3], m_lat[4]), router_grp[l], router_grp_b[l],
            router_exp[l], router_exp_b[l], moe_w_gate[l], moe_w_up[l], moe_w_down[l])
        if not last:
            h_ctx = h_ctx + m_ctx[2] * y_ctx
            h_ctx = h_ctx + m_ctx[5] * hier_moe(
                modulate(rmsnorm(h_ctx, norm_ffn_g[l]), m_ctx[3], m_ctx[4]), router_grp[l], router_grp_b[l],
                router_exp[l], router_exp_b[l], moe_w_gate[l], moe_w_up[l], moe_w_down[l])
    return rmsnorm(h_lat, final_norm_g)


def setup_inputs(seed=0):
    out = dict(first_inputs(seed))
    for name, value in second_inputs(seed + 1).items():
        if name != "x":
            out[name + "_2"] = value
    return out


def reference(
    x, rel_bias, norm_mix, w_in, a_q_norm, a_k_norm, b_cq_norm, b_ckv_norm, b_w_uq, b_w_ukv,
    b_q_norm, b_k_norm, w_proj_a, w_proj_b, b_gate, w_out, norm_ffn, w_up, conv_w, conv_b,
    w_down, c_2, ctx_2, c_ctx_2, ada_w_2, ada_b_2, norm_mix_g_2, norm_ffn_g_2, w_in_2,
    gdn_conv_2, gdn_a_log_2, gdn_dt_bias_2, gdn_onorm_g_2, rwkv_mu_2, rwkv_w0_2, rwkv_w2_2,
    rwkv_a0_2, rwkv_a2_2, rwkv_g2_2, rwkv_k_k_2, rwkv_k_a_2, rwkv_r_k_2, rwkv_lnx_g_2,
    rwkv_lnx_b_2, w_o_a_2, w_o_b_2, w_out_2, router_grp_2, router_grp_b_2, router_exp_2,
    router_exp_b_2, moe_w_gate_2, moe_w_up_2, moe_w_down_2, final_norm_g_2,
):
    x = first_block(
        x, rel_bias, norm_mix, w_in, a_q_norm, a_k_norm, b_cq_norm, b_ckv_norm, b_w_uq, b_w_ukv,
        b_q_norm, b_k_norm, w_proj_a, w_proj_b, b_gate, w_out, norm_ffn, w_up, conv_w, conv_b,
        w_down,
    )
    return second_block(
        x, c_2, ctx_2, c_ctx_2, ada_w_2, ada_b_2, norm_mix_g_2, norm_ffn_g_2, w_in_2,
        gdn_conv_2, gdn_a_log_2, gdn_dt_bias_2, gdn_onorm_g_2, rwkv_mu_2, rwkv_w0_2, rwkv_w2_2,
        rwkv_a0_2, rwkv_a2_2, rwkv_g2_2, rwkv_k_k_2, rwkv_k_a_2, rwkv_r_k_2, rwkv_lnx_g_2,
        rwkv_lnx_b_2, w_o_a_2, w_o_b_2, w_out_2, router_grp_2, router_grp_b_2, router_exp_2,
        router_exp_b_2, moe_w_gate_2, moe_w_up_2, moe_w_down_2, final_norm_g_2,
    )


_drawn_inputs = setup_inputs


def setup_inputs(seed=0):
    import zlib

    import numpy as np

    out = dict(_drawn_inputs(seed))
    spreads = {}
    factors = {'rel_bias': 2.832,
     'a_q_norm': 8.0,
     'a_k_norm': 6.389,
     'b_cq_norm': 8.0,
     'b_ckv_norm': 7.262,
     'b_q_norm': 8.0,
     'b_k_norm': 8.0,
     'b_gate': 8.0,
     'conv_b': 3.935,
     'c_ctx_2': 23.728,
     'ada_b_2': 6.837,
     'norm_mix_g_2': 5.797,
     'norm_ffn_g_2': 23.212,
     'gdn_a_log_2': 4.444,
     'gdn_onorm_g_2': 49.494,
     'rwkv_w2_2': 36.0,
     'rwkv_a0_2': 8.0,
     'rwkv_a2_2': 3.142,
     'rwkv_k_k_2': 53.176,
     'rwkv_k_a_2': 6.174,
     'rwkv_lnx_g_2': 64.0,
     'rwkv_lnx_b_2': 200.0,
     'router_grp_b_2': 200.0,
     'router_exp_b_2': 64.0,
     'ctx_2': 8.0,
     'rwkv_w0_2': 8.0}
    for name, (base, spread) in spreads.items():
        noise = np.random.default_rng([zlib.crc32(name.encode()), seed]).standard_normal(out[name].shape)
        drawn = base * np.exp(spread * noise) if base else spread * noise
        out[name] = __import__('jax').numpy.asarray(drawn.astype(out[name].dtype))
    for name, factor in factors.items():
        out[name] = (out[name] * factor).astype(out[name].dtype)
    return out
```

```python
import math
from contextlib import ExitStack
from itertools import chain, zip_longest

import concourse.bass as bass
import numpy as np
from concourse import mybir

ALU = mybir.AluOpType
ACT_F = mybir.ActivationFunctionType
AX = mybir.AxisListType.X
F32 = mybir.dt.float32
U8 = mybir.dt.uint8

P = 128
D = 1024
KD = D // P
S = 256
TT = S // P
DEPTH = 2
HEADS = 8
HD = 64
TOPK = 64
QK_B = 96
ROPE = 32
Q_LORA = 384
KV_LORA = 256
D_FF = 2816
FT = D_FF // P
IN1 = 4840
EPS = 1e-6
HIDDEN = -1e30
TAKEN = -3e38
Z_QA, Z_KA, Z_VA, Z_QI, Z_KI, Z_WI, Z_CQ, Z_CKV, Z_KR, Z_GA, Z_GB = (
    0, 512, 1024, 1536, 2048, 2112, 2120, 2504, 2760, 2792, 3816)

DELTA_CHAINS = tuple((h, 1, (2 * h, 2 * h + 1)) for h in range(4))

T2 = 4
B_COLS = 1920
GDN_H = 4
RH = 8
N_EXP = 32
CH = 64
LEVELS = 6

SLAB = 4096
NSLOT = 3
K_ORDER = (3, 6, 2, 5, 7, 0, 1, 4)


def slab_sizes():
    out = []
    for _ in range(DEPTH):
        out += [KD * 512] * (IN1 // 512) + [KD * (IN1 % 512)]
        out += [4 * KD * P] * 2 + [3 * 768, 2 * 1024] + [4 * KD * P] * (12 // DEPTH - 2)
        out += [4 * 1024, 4 * 1024, KD * 512, KD * 512]
        out += [4 * KD * P] * (2 * FT // 4)
        out += [4 * D] * (FT // 4) + [(FT % 4) * D]
    out += [KD * 512] * 3 + [KD * 384]
    out += [4 * KD * P] * 3 + [KD * 512, KD * 16]
    out += [KD * 512] * 4 + [4 * D, 4 * D, KD * 512, KD * 512, KD * 36]
    out += [4 * KD * P, 4 * KD * P, 2 * 2 * D] * (N_EXP // 2)
    return out


def offsets(parts):
    out, at = {}, 0
    for name, n in parts:
        out[name] = at
        at += n
    out["all"] = at
    return out


COL = offsets([(f"{n}{l}", w) for l in range(DEPTH) for n, w in (
    ("mix", KD), ("ffn", KD), ("aq", 1), ("ak", 1), ("cq", 3), ("ckv", 2), ("bq", 1), ("bk", 1),
    ("conv", 4 * 2 * FT))] + [("ada_b", 48), ("c", KD), ("cc", KD), ("mix2", KD), ("ffn2", KD), ("gconv", 60)])
ROW = offsets([("mu", B_COLS), ("w0", 1024), ("a0", 1024), ("k_k", 512), ("k_a", 512), ("r_k", 512),
               ("lnx_g", 512), ("lnx_b", 512), ("a_log", 8), ("dt", 8), ("onorm", 128), ("rb", 36), ("fin", D)])
K1 = offsets([("ident", P), ("cos", TT * 16), ("sin", TT * 16), ("hidden", TT * S), ("bucket", 2 * S - 1), ("flip", P)])
K2 = offsets([("index", 8), ("shift", P), ("shift_n", P), ("shift_p", P), ("ones", P), ("reset16", T2 * P), ("reset4", T2 * P // 16)]
             + [(f"{n}{d}", w) for d in range(2) for n, w in (
                 ("cum", P), ("cumx", P), ("nstrict", P), ("nstrictT", P), ("strictT", P), ("inclT", P),
                 ("col4", 4), ("level", LEVELS * P), ("last", P))])


def constants():
    k1 = np.zeros((P, K1["all"]), np.float32)
    k1[:, K1["ident"]:K1["ident"] + P] = np.eye(P)
    k1[:, K1["flip"]:K1["flip"] + P] = np.eye(P)[::-1]
    half = ROPE // 2
    inv = np.float32(10000.0) ** (-np.arange(half, dtype=np.float32) / np.float32(half))
    ang = np.arange(S, dtype=np.float32)[:, None] * inv[None, :]
    for m in range(TT):
        k1[:, K1["cos"] + m * 16:K1["cos"] + m * 16 + 16] = np.cos(ang[m * P:(m + 1) * P])
        k1[:, K1["sin"] + m * 16:K1["sin"] + m * 16 + 16] = np.sin(ang[m * P:(m + 1) * P])
        tq = m * P + np.arange(P)
        ok = (np.arange(S)[None, :] // 64) <= (tq // 64)[:, None]
        k1[:, K1["hidden"] + m * S:K1["hidden"] + (m + 1) * S] = np.where(ok, 0.0, HIDDEN)
    rel = np.arange(-(S - 1), S)
    n = np.abs(rel)
    nf = np.maximum(n, 1).astype(np.float32)
    large = 8 + (np.log(nf / np.float32(8)) / np.float32(math.log(128 / 8)) * np.float32(8)).astype(np.int32)
    bucket = np.where(rel > 0, 16, 0) + np.where(n < 8, n, np.minimum(large, 15))
    k1[bucket, K1["bucket"] + np.arange(2 * S - 1)] = 1.0

    k2 = np.zeros((P, K2["all"]), np.float32)
    s, t = np.arange(P)[:, None], np.arange(P)[None, :]

    def put(name, a):
        k2[:, K2[name]:K2[name] + a.shape[1]] = a

    put("shift", 0.5 * (np.abs(s - t) == 1) - 1.0 * (s == t))
    put("shift_n", 0.5 * ((s == 0) & (t == P - 1)))
    put("shift_p", 0.5 * ((s == P - 1) & (t == 0)))
    put("ones", np.ones((P, P)))
    put("index", np.broadcast_to(np.arange(8.0), (P, 8)))
    put("reset16", np.broadcast_to(1.0 * (np.arange(T2 * P) % 16 != 0), (P, T2 * P)))
    put("reset4", np.broadcast_to(1.0 * (np.arange(T2 * P // 16) % 4 != 0), (P, T2 * P // 16)))
    for d in range(2):
        before = (s < t) if d == 0 else (s > t)
        same = s // CH == t // CH
        ps, pt = s % CH, t % CH
        early = (ps < CH // 2) if d == 0 else (ps >= CH // 2)
        incl = (before | (s == t)) & same
        put(f"cum{d}", 1.0 * incl - 1.0 * (early & same))
        put(f"cumx{d}", 1.0 * (before & same) - 1.0 * (early & same))
        put(f"nstrict{d}", -1.0 * (before & same).T)
        put(f"nstrictT{d}", -1.0 * (before & same))
        put(f"strictT{d}", 1.0 * (before & same))
        put(f"inclT{d}", 1.0 * incl)
        c4 = np.zeros((P, 4))
        for c in range(2):
            inside = (s[:, 0] // CH) == c
            c4[:, 2 * c] = inside & early[:, 0]
            c4[:, 2 * c + 1] = inside & ~early[:, 0]
        put(f"col4{d}", c4)
        lv = np.zeros((P, LEVELS * P))
        for level in range(LEVELS):
            b = 2 ** level
            off = (s // b != t // b) & (s // (2 * b) == t // (2 * b)) & before.T
            lv[:, level * P:(level + 1) * P] = 1.0 * (s == t) - 1.0 * off
        put(f"level{d}", lv)
        put(f"last{d}", 1.0 * ((s % CH == (CH - 1 if d == 0 else 0)) & same))
    return k1, k2


class Count:

    def __init__(self):
        self.pe = self.dve = self.act = self.pool = self.sp = 0
        self.slab = 0
        self.bank = 0

    def of(self, name):
        return {"pe": self.pe, "dve": self.dve, "act": self.act, "pool": self.pool}[name]


class Carve:

    def __init__(self, base, at=0):
        self.base, self.at = base, at

    def __call__(self, *dims):
        n = int(np.prod(dims))
        out = self.base[:, self.at:self.at + n]
        self.at += n
        assert self.at <= self.base.shape[1], (self.at, self.base.shape)
        if len(dims) == 2:
            out = out.rearrange("p (a b) -> p a b", a=dims[0])
        elif len(dims) == 3:
            out = out.rearrange("p (a b c) -> p a b c", a=dims[0], b=dims[1])
        elif len(dims) == 4:
            out = out.rearrange("p (a b c d) -> p a b c d", a=dims[0], b=dims[1], c=dims[2])
        return out


ARENA = 36928


def build(nc, stream, cols, rows, k1, k2, lora, x_in, ctx_in, rel_bias, out):
    sizes = slab_sizes()
    starts = np.concatenate([[0], np.cumsum(sizes)]).tolist()
    with ExitStack() as ctx:
        def sb(name, shape, dt=F32):
            return ctx.enter_context(nc.sbuf_tensor(name, shape, dt))

        def sem(name):
            return ctx.enter_context(nc.semaphore(name))

        ring = sb("weight_ring", [P, NSLOT, SLAB])
        x = sb("residual", [P, TT, D])
        kc = sb("constants", [P, K1["flip"]])
        cc = sb("columns", [P, COL["all"]])
        ss = sb("square_sums", [P, 64])
        arena = sb("arena", [P, ARENA])
        conds = sb("conditions", [P, KD, 2])
        mod = sb("modulation", [P, 48, 2])
        bank = [ctx.enter_context(nc.psum_tensor(f"bank{i}", [P, 512], F32)) for i in range(8)]
        bias_dram = nc.dram_tensor("bias_rows", (HEADS, 2 * S - 1), F32, kind="Internal").ap()

        u_dram = nc.dram_tensor("u_rest", (P, KD, T2 * P), F32, kind="Internal").ap()

        slab_full = [sem(f"slab_full{i}") for i in range(NSLOT)]
        loaded = sem("small_loads_done")
        stored = sem("stores_done")
        spilled = sem("u_spilled")
        pe_done, dve_done, act_done, pool_done = sem("pe_done"), sem("dve_done"), sem("act_done"), sem("pool_done")
        dve_link, act_link, pool_link = sem("dve_link"), sem("act_link"), sem("pool_link")

        ident = kc[:, K1["ident"]:K1["ident"] + P]

        def col(name, n=1, at=0):
            return cc[:, COL[name] + at:COL[name] + at + n]

        def program(PE=None, DVE=None, ACT=None, POOL=None, SP=None):
            c = Count()
            links = {"dve": 0, "act": 0, "pool": 0}
            bank_free = [None] * 8
            done = {"pe": pe_done, "dve": dve_done, "act": act_done, "pool": pool_done}

            def link(ins):
                if DVE:
                    links["dve"] += 1
                    ins.then_inc(dve_link, 1)
                    DVE.wait_ge(dve_link, links["dve"])
                if ACT:
                    links["act"] += 1
                    ins.then_inc(act_link, 1)
                    ACT.wait_ge(act_link, links["act"])
                if POOL:
                    links["pool"] += 1
                    ins.then_inc(pool_link, 1)
                    POOL.wait_ge(pool_link, links["pool"])

            def settle(eng):
                for name in ("pe", "dve", "act", "pool"):
                    if c.of(name):
                        eng.wait_ge(done[name], c.of(name))
                if c.sp:
                    eng.wait_ge(loaded, 16 * c.sp)

            def take(b):
                if PE and bank_free[b]:
                    PE.wait_ge(done[bank_free[b][0]], bank_free[b][1])
                return bank[b]

            def turn(n=8, first=0):
                c.bank += 1
                return first + c.bank % n

            def load_slab(i):
                if SP and i < len(sizes):
                    n = sizes[i]
                    SP.dma_start(ring[:, i % NSLOT, 0:n], stream[:, starts[i]:starts[i] + n])\
                        .then_inc(slab_full[i % NSLOT], 16)

            def open_slab():
                i = c.slab
                if PE:
                    PE.wait_ge(slab_full[i % NSLOT], 16 * (i // NSLOT + 1))
                return ring[:, i % NSLOT, 0:sizes[i]]

            def close_slab():
                if SP:
                    SP.wait_ge(pe_done, c.pe)
                load_slab(c.slab + NSLOT)
                c.slab += 1

            def load(dst, src):
                if SP:
                    settle(SP)
                    SP.dma_start(dst, src).then_inc(loaded, 16)
                c.sp += 1

            def read_out(b, fn_act=None, fn_dve=None):
                m = c.pe
                if fn_act:
                    if ACT:
                        ACT.wait_ge(pe_done, m)
                        fn_act().then_inc(act_done, 1)
                    c.act += 1
                    bank_free[b] = ("act", c.act)
                else:
                    if DVE:
                        DVE.wait_ge(pe_done, m)
                        fn_dve().then_inc(dve_done, 1)
                    c.dve += 1
                    bank_free[b] = ("dve", c.dve)

            def copy_out(b, dst, src):
                if b % 2:
                    read_out(b, fn_act=lambda: nc.scalar.activation(dst, src, ACT_F.Copy))
                else:
                    read_out(b, fn_dve=lambda: nc.vector.tensor_copy(dst, src))

            def scale_from_squares(n, per):
                if DVE:
                    DVE.wait_ge(act_done, c.act)
                    DVE.wait_ge(dve_done, c.dve)
                    nc.vector.tensor_scalar(ss[:, 0:n], ss[:, 0:n], 1.0 / per, EPS, ALU.mult, ALU.add)\
                        .then_inc(dve_done, 1)
                c.dve += 1
                if ACT:
                    ACT.wait_ge(dve_done, c.dve)
                    nc.scalar.activation(ss[:, 0:n], ss[:, 0:n], ACT_F.Sqrt).then_inc(act_done, 1)
                c.act += 1
                if DVE:
                    DVE.wait_ge(act_done, c.act)
                    nc.vector.reciprocal(ss[:, 0:n], ss[:, 0:n]).then_inc(dve_done, 1)
                c.dve += 1

            def norm_heads(src, dst, sq, heads, per, n=None):
                if DVE:
                    settle(DVE)
                    link(nc.vector.tensor_tensor(sq, src, src, ALU.mult))
                    nc.vector.tensor_reduce(ss[:, 0:heads], sq, AX, ALU.add).then_inc(dve_done, 1)
                c.dve += 1
                scale_from_squares(heads, per)
                if DVE:
                    DVE.wait_ge(dve_done, c.dve)
                    w = src.shape[2]
                    nc.vector.tensor_tensor(dst, src, ss[:, 0:heads].unsqueeze(2).to_broadcast([P, heads, w]),
                                            ALU.mult).then_inc(dve_done, 1)
                c.dve += 1

            def norm_rows(src, xn, tiles):
                if ACT:
                    settle(ACT)
                    for m in range(tiles):
                        link(nc.scalar.activation(xn[:, m, :], src[:, m, :], ACT_F.Square,
                                                  accum_out=ss[:, m:m + 1]))
                    nc.scalar.activation(xn[:, 0, 0:1], xn[:, 0, 0:1], ACT_F.Copy).then_inc(act_done, 1)
                c.act += 1
                scale_from_squares(tiles, D)
                if DVE:
                    DVE.wait_ge(dve_done, c.dve)
                    for m in range(tiles):
                        last = nc.vector.tensor_scalar(xn[:, m, :], src[:, m, :], ss[:, m:m + 1], None, ALU.mult)
                    last.then_inc(dve_done, 1)
                c.dve += 1

            def transposes(jobs, tiles=2, nb=8):
                if PE:
                    settle(PE)
                per = 4 // tiles
                for at in range(0, len(jobs), per):
                    group = jobs[at:at + per]
                    b = turn(nb)
                    take(b)
                    if PE:
                        for j, (src, dst, n, scale, bias) in enumerate(group):
                            for m in range(tiles):
                                last = nc.tensor.transpose(bank[b][0:n, (j * tiles + m) * P:(j * tiles + m + 1) * P],
                                                           src(m), ident)
                        last.then_inc(pe_done, 1)
                    c.pe += 1

                    def by_act():
                        for j, (src, dst, n, scale, bias) in enumerate(group):
                            bb = bank[b][0:n, j * tiles * P:(j + 1) * tiles * P]
                            if len(dst.shape) == 3:
                                bb = bb.rearrange("p (a b) -> p a b", b=dst.shape[2])
                            last = nc.scalar.activation(dst, bb, ACT_F.Identity if scale is not None else ACT_F.Copy,
                                                        **({"scale": scale} if scale is not None else {}),
                                                        **({"bias": bias} if bias is not None else {}))
                        return last

                    def by_dve():
                        for j, (src, dst, n, scale, bias) in enumerate(group):
                            bb = bank[b][0:n, j * tiles * P:(j + 1) * tiles * P]
                            if len(dst.shape) == 3:
                                bb = bb.rearrange("p (a b) -> p a b", b=dst.shape[2])
                            if scale is None:
                                last = nc.vector.tensor_copy(dst, bb)
                            elif bias is None:
                                last = nc.vector.tensor_scalar(dst, bb, scale, None, ALU.mult)
                            else:
                                last = nc.vector.tensor_scalar(dst, bb, scale, bias, ALU.mult, ALU.add)
                        return last

                    if b % 2:
                        read_out(b, fn_act=by_act)
                    else:
                        read_out(b, fn_dve=by_dve)

            def rows_product(left, kt, tiles, widths, read, nb=8, order=None):
                if PE:
                    settle(PE)
                for s, n in enumerate(widths):
                    w = open_slab()
                    for h0 in range(0, n, 512):
                        nn = min(512, n - h0)
                        for m in tiles:
                            b = turn(nb)
                            take(b)
                            if PE:
                                for j, k in enumerate(order or range(kt)):
                                    last = nc.tensor.matmul(bank[b][:, 0:nn], left(k, m),
                                                            w[:, k * n + h0:k * n + h0 + nn],
                                                            start=(j == 0), stop=(j == kt - 1))
                                last.then_inc(pe_done, 1)
                            c.pe += 1
                            read(m, s, h0, nn, b)
                    close_slab()

            def same_half(u):
                h = 4 * (u // 2) + u % 2
                return HD * (u % 2), (h, h + 2)

            if SP:
                SP.dma_start(kc[:, :], k1[:, 0:K1["flip"]]).then_inc(loaded, 16)
                SP.dma_start(cc[:, :], cols).then_inc(loaded, 16)
                SP.dma_start(x[:, :, :], x_in.rearrange("b (m p) d -> p (b m) d", p=P)).then_inc(loaded, 16)
                SP.dma_start(ss[0:32, 0:HEADS], rel_bias).then_inc(loaded, 16)
            c.sp += 4
            for i in range(NSLOT):
                load_slab(i)

            b = turn()
            take(b)
            if PE:
                settle(PE)
                nc.tensor.matmul(bank[b][0:HEADS, 0:2 * S - 1], ss[0:32, 0:HEADS],
                                 kc[0:32, K1["bucket"]:K1["bucket"] + 2 * S - 1], start=True, stop=True)\
                    .then_inc(pe_done, 1)
            c.pe += 1
            tab = Carve(arena)
            rows_sb = tab(2 * S - 1)
            read_out(b, fn_dve=lambda: nc.vector.tensor_copy(rows_sb[0:HEADS, :], bank[b][0:HEADS, 0:2 * S - 1]))
            load(bias_dram, rows_sb[0:HEADS, :])

            get = Carve(arena, 512)
            bias = get(TT, HEADS, S)
            gate_bias = get(2 * D)
            z = get(TT, IN1)
            hT = get(KD, S)
            kbT = get(HEADS, S)
            qaT, kaT, qiT, kiT = get(4, S), get(4, S), get(4, S), get(1, S)
            cqT, ckvT = get(3, S), get(2, S)
            kv = get(TT, D)
            kb = get(TT, HEADS, QK_B)
            score, selm = get(TT, S), get(TT, S)
            yT = [get(4, S), get(4, S)]
            kidup = get(TT, 2, HD)
            wi = get(TT, HEADS)
            work = get(2 * D)
            top8 = get(TT, 8)
            mx = get(4, 2)
            assert get.at <= ARENA, get.at
            qbT = hT
            hid = z.rearrange("p a b -> p (a b)")[:, 0:FT * S].rearrange("p (a b) -> p a b", a=FT)
            falling = z.rearrange("p a b -> p (a b)")[:, 0:TT * HEADS * S].rearrange("p (m h s) -> p m h s", m=TT, h=HEADS)
            flip = work[:, 0:P]
            if SP:
                settle(SP)
                for m in range(TT):
                    SP.dma_start(falling[:, m, :, :], bass.AP(tensor=bias_dram.tensor, offset=S - 1 - m * P - (P - 1),
                                                              ap=[[1, P], [2 * S - 1, HEADS], [1, S]])).then_inc(loaded, 16)
                SP.dma_start(flip, k1[:, K1["flip"]:K1["flip"] + P]).then_inc(loaded, 16)
            c.sp += TT + 1
            if PE:
                settle(PE)
            for m in range(TT):
                for h in range(0, HEADS, 2):
                    b = turn()
                    take(b)
                    if PE:
                        nc.tensor.matmul(bank[b][:, :], flip,
                                         falling[:, m, h:h + 2, :].rearrange("p h s -> p (h s)"),
                                         start=True, stop=True).then_inc(pe_done, 1)
                    c.pe += 1
                    copy_out(b, bias[:, m, h:h + 2, :].rearrange("p h s -> p (h s)"), bank[b][:, :])

            if ACT:
                settle(ACT)
                nc.scalar.activation(conds[:, :, 0], col("c", KD), ACT_F.Silu)
                nc.scalar.activation(conds[:, :, 1], col("cc", KD), ACT_F.Silu).then_inc(act_done, 1)
            c.act += 1

            def modulation(s):
                w = open_slab()
                b = 6 + s % 2
                take(b)
                for t in range(4):
                    for part in range(2):
                        if PE:
                            for k in range(4 * part, 4 * part + 4):
                                last = nc.tensor.matmul(bank[b][:, 2 * t:2 * t + 2],
                                                        w[:, (t * KD + k) * P:(t * KD + k + 1) * P],
                                                        conds[:, k, :], start=(k == 0), stop=(k == KD - 1))
                            if t == 3 and part == 1:
                                last.then_inc(pe_done, 1)
                        if t < 3 or part < 1:
                            yield
                c.pe += 1
                close_slab()
                read_out(b, fn_dve=lambda: nc.vector.tensor_tensor(
                    mod[:, 4 * s:4 * s + 4, :], bank[b][:, 0:8].rearrange("p (a b) -> p a b", a=4),
                    col("ada_b", 4, 4 * s).unsqueeze(2).to_broadcast([P, 4, 2]), ALU.add))
                yield

            for l in range(DEPTH):
                load(gate_bias, rows[0:1, l * 2 * D:(l + 1) * 2 * D].to_broadcast([P, 2 * D]))
                xn = work.rearrange("p (m d) -> p m d", m=TT)
                norm_rows(x, xn, TT)
                transposes([(lambda m, k=k: xn[:, m, k * P:(k + 1) * P], hT[:, k, :], P, col(f"mix{l}", 1, k), None)
                            for k in range(KD)])
                rows_product(lambda k, m: hT[:, k, m * P:(m + 1) * P], KD, range(TT),
                             [512] * (IN1 // 512) + [IN1 % 512],
                             lambda m, s, h0, n, b: copy_out(b, z[:, m, 512 * s:512 * s + n], bank[b][:, 0:n]), order=K_ORDER)
                if POOL:
                    settle(POOL)
                    for m in range(TT):
                        last = nc.gpsimd.tensor_tensor(z[:, m, Z_GA:Z_GA + 2 * D], z[:, m, Z_GA:Z_GA + 2 * D],
                                                       gate_bias, ALU.add)
                        link(nc.gpsimd.tensor_copy(kidup[:, m, :, :], z[:, m, Z_KI:Z_KI + HD].unsqueeze(1)
                                                   .to_broadcast([P, 2, HD])))
                    nc.gpsimd.tensor_copy(wi[:, 0, 0:1], z[:, 0, Z_WI:Z_WI + 1]).then_inc(pool_done, 1)
                c.pool += 1
                for m in range(TT):
                    zq = z[:, m, 0:1024].rearrange("p (h d) -> p h d", d=HD)
                    norm_heads(zq, zq, work[:, 0:1024].rearrange("p (h d) -> p h d", d=HD), 16, HD)
                    for at, n in ((Z_CQ, Q_LORA), (Z_CKV, KV_LORA)):
                        zc = z[:, m, at:at + n].unsqueeze(1)
                        norm_heads(zc, zc, work[:, 0:n].unsqueeze(1), 1, n)
                if ACT:
                    settle(ACT)
                    for m in range(TT):
                        last = nc.scalar.activation(z[:, m, Z_GA:Z_GA + 2 * D], z[:, m, Z_GA:Z_GA + 2 * D],
                                                    ACT_F.Sigmoid)
                    last.then_inc(act_done, 1)
                c.act += 1
                slabs = iter(range(12 // DEPTH * l, 12 // DEPTH * (l + 1)))
                for _ in range(2):
                    for _ in modulation(next(slabs)):
                        pass
                blk = lambda base, n=P: (lambda m: z[:, m, base:base + n])
                transposes([(blk(Z_QA + P * i), qaT[:, i, :], P, col(f"aq{l}"), None) for i in range(4)]
                           + [(blk(Z_KA + P * i), kaT[:, i, :], P, col(f"ak{l}"), None) for i in range(4)]
                           + [(blk(Z_QI + P * i), qiT[:, i, :], P, None, None) for i in range(4)]
                           + [(lambda m: kidup[:, m, :, :].rearrange("p a b -> p (a b)"), kiT[:, 0, :], P, None, None)]
                           + [(blk(Z_CQ + P * i), cqT[:, i, :], P, col(f"cq{l}", 1, i), None) for i in range(3)]
                           + [(blk(Z_CKV + P * i), ckvT[:, i, :], P, col(f"ckv{l}", 1, i), None) for i in range(2)])
                if PE:
                    settle(PE)
                rows_product(lambda k, m: cqT[:, k, m * P:(m + 1) * P], 3, range(TT), [768],
                             lambda m, s, h0, n, b: copy_out(b, z[:, m, h0:h0 + n], bank[b][:, 0:n]))
                rows_product(lambda k, m: ckvT[:, k, m * P:(m + 1) * P], 2, range(TT), [1024],
                             lambda m, s, h0, n, b: copy_out(b, kv[:, m, h0:h0 + n], bank[b][:, 0:n]))
                if DVE:
                    settle(DVE)
                    for m in range(TT):
                        qv = z[:, m, 0:768].rearrange("p (h d) -> p h d", d=QK_B)
                        kr = z[:, m, Z_KR:Z_KR + ROPE].unsqueeze(1)
                        for v, base, h in ((qv, 64, HEADS), (kr, 0, 1)):
                            cs = kc[:, K1["cos"] + 16 * m:K1["cos"] + 16 * m + 16].unsqueeze(1).to_broadcast([P, h, 16])
                            sn = kc[:, K1["sin"] + 16 * m:K1["sin"] + 16 * m + 16].unsqueeze(1).to_broadcast([P, h, 16])
                            x1, x2 = v[:, :, base:base + 16], v[:, :, base + 16:base + 32]
                            t = [work[:, 128 * i:128 * i + 16 * h].rearrange("p (h d) -> p h d", d=16) for i in range(4)]
                            nc.vector.tensor_tensor(t[0], x1, cs, ALU.mult)
                            nc.vector.tensor_tensor(t[1], x2, sn, ALU.mult)
                            nc.vector.tensor_tensor(t[2], x1, sn, ALU.mult)
                            link(nc.vector.tensor_tensor(t[3], x2, cs, ALU.mult))
                            nc.vector.tensor_tensor(x1, t[0], t[1], ALU.subtract)
                            link(nc.vector.tensor_tensor(x2, t[2], t[3], ALU.add))
                        kvm = kv[:, m, :].rearrange("p (h d) -> p h d", d=P)
                        nc.vector.tensor_copy(kb[:, m, :, 0:HD], kvm[:, :, 0:HD])
                        last = nc.vector.tensor_copy(kb[:, m, :, HD:QK_B], kr.to_broadcast([P, HEADS, ROPE]))
                    last.then_inc(dve_done, 1)
                c.dve += 1
                for m in range(TT):
                    qv = z[:, m, 0:768].rearrange("p (h d) -> p h d", d=QK_B)
                    sq = work[:, 0:768].rearrange("p (h d) -> p h d", d=QK_B)
                    norm_heads(qv, qv, sq, HEADS, QK_B)
                    norm_heads(kb[:, m, :, :], kb[:, m, :, :], sq, HEADS, QK_B)
                for _ in modulation(next(slabs)):
                    pass
                transposes([(blk(QK_B * i, QK_B), qbT[0:QK_B, i, :], QK_B, col(f"bq{l}")[0:QK_B], None)
                            for i in range(HEADS)]
                           + [(lambda m, i=i: kb[:, m, i, :], kbT[0:QK_B, i, :], QK_B, col(f"bk{l}")[0:QK_B], None)
                              for i in range(HEADS)])
                if DVE:
                    settle(DVE)
                    for m in range(TT):
                        last = nc.vector.tensor_scalar(wi[:, m, :], z[:, m, Z_WI:Z_WI + HEADS],
                                                       HEADS ** -0.5 * HD ** -0.5, None, ALU.mult)
                    last.then_inc(dve_done, 1)
                c.dve += 1
                rel = work.rearrange("p (a h s) -> p a h s", a=4, h=2)
                rel_used = {}
                if PE:
                    settle(PE)
                if ACT:
                    settle(ACT)
                for i in range(2 * 4):
                    m, u = divmod(i, 4)
                    base, heads = same_half(u)
                    b = turn()
                    take(b)
                    if PE:
                        for j, h in enumerate(heads):
                            last = nc.tensor.matmul(bank[b][:, j * S:(j + 1) * S],
                                                    qiT[base:base + HD, h // 2, m * P:(m + 1) * P],
                                                    kiT[base:base + HD, 0, :], start=True, stop=True)
                        last.then_inc(pe_done, 1)
                    c.pe += 1
                    r = rel[:, i % 4, :, :]
                    if ACT:
                        if i >= 4:
                            ACT.wait_ge(dve_done, rel_used[i - 4])
                        ACT.wait_ge(pe_done, c.pe)
                        nc.scalar.activation(r, bank[b][:, :].rearrange("p (h s) -> p h s", h=2), ACT_F.Relu)\
                            .then_inc(act_done, 1)
                    c.act += 1
                    bank_free[b] = ("act", c.act)
                    if DVE:
                        DVE.wait_ge(act_done, c.act)
                        for j, h in enumerate(heads):
                            if h == 0:
                                link(nc.vector.tensor_scalar(score[:, m, :], r[:, j, :], wi[:, m, h:h + 1], None, ALU.mult))
                            elif j == 0:
                                link(nc.vector.scalar_tensor_tensor(score[:, m, :], r[:, j, :], wi[:, m, h:h + 1],
                                                                    score[:, m, :], ALU.mult, ALU.add))
                            else:
                                last = nc.vector.scalar_tensor_tensor(score[:, m, :], r[:, j, :], wi[:, m, h:h + 1],
                                                                      score[:, m, :], ALU.mult, ALU.add)
                        last.then_inc(dve_done, 1)
                        DVE.wait_ge(dve_done, c.dve + 1)
                    c.dve += 1
                    rel_used[i] = c.dve
                if DVE:
                    for m in range(TT):
                        hidden = kc[:, K1["hidden"] + m * S:K1["hidden"] + (m + 1) * S]
                        link(nc.vector.tensor_tensor(score[:, m, :], score[:, m, :], hidden, ALU.add))
                    for r in range(TOPK // 8):
                        for m in range(TT):
                            last = nc.vector.max(top8[:, m, :], score[:, m, :])
                        link(last)
                        for m in range(TT):
                            last = nc.vector.match_replace(score[:, m, :], top8[:, m, :], score[:, m, :], TAKEN)
                        link(last)
                    for m in range(TT):
                        last = nc.vector.tensor_scalar(selm[:, m, :], score[:, m, :], TAKEN / 2, HIDDEN,
                                                       ALU.is_gt, ALU.mult)
                    last.then_inc(dve_done, 1)
                c.dve += 1
                for _ in modulation(next(slabs)):
                    pass
                logits_m, prob_m, turned_m, copied_m, outs_m = {}, {}, {}, {}, {}
                units = [(br, m, u) for br in range(2) for m in range(TT) for u in range(4)]
                pr = [work[:, 512 * i:512 * i + 512].rearrange("p (h s) -> p h s", h=2) for i in range(2)]
                pT = [work[:, 1024 + 512 * i:1536 + 512 * i] for i in range(2)]
                if PE:
                    settle(PE)
                if ACT:
                    settle(ACT)
                if DVE:
                    settle(DVE)

                def logits(i):
                    br, m, u = units[i]
                    base, heads = same_half(u)
                    b = i % 2
                    take(b)
                    if PE:
                        for j, h in enumerate(heads):
                            if br == 0:
                                q, k = qaT[base:base + HD, h // 2, m * P:(m + 1) * P], kaT[base:base + HD, h // 2, :]
                            else:
                                q, k = qbT[0:QK_B, h, m * P:(m + 1) * P], kbT[0:QK_B, h, :]
                            last = nc.tensor.matmul(bank[b][:, j * S:(j + 1) * S], q, k, start=True, stop=True)
                        last.then_inc(pe_done, 1)
                    c.pe += 1
                    logits_m[i] = c.pe

                def softmax(i):
                    br, m, u = units[i]
                    base, heads = same_half(u)
                    p, b = pr[i % 2], i % 2
                    if DVE:
                        DVE.wait_ge(pe_done, logits_m[i])
                        if i >= 2:
                            DVE.wait_ge(pe_done, turned_m[i - 2])
                        lg = bank[b][:, :].rearrange("p (h s) -> p h s", h=2)
                        if br == 0:
                            link(nc.vector.scalar_tensor_tensor(p, lg, HD ** -0.5, bias[:, m, heads[0]:heads[1] + 1:2, :],
                                                                ALU.mult, ALU.add))
                            mask = selm[:, m, :]
                            link(nc.vector.tensor_tensor(p, p, mask.unsqueeze(1).to_broadcast([P, 2, S]), ALU.add))
                        else:
                            mask = kc[:, K1["hidden"] + m * S:K1["hidden"] + (m + 1) * S]
                            link(nc.vector.scalar_tensor_tensor(p, lg, QK_B ** -0.5,
                                                                mask.unsqueeze(1).to_broadcast([P, 2, S]),
                                                                ALU.mult, ALU.add))
                        link(nc.vector.tensor_reduce(mx[:, i % 2, :], p, AX, ALU.max))
                        nc.vector.tensor_scalar(mx[:, i % 2, :], mx[:, i % 2, :], -1.0, None, ALU.mult)\
                            .then_inc(dve_done, 1)
                    c.dve += 1
                    bank_free[b] = ("dve", c.dve)
                    if ACT:
                        ACT.wait_ge(dve_done, c.dve)
                        for j in range(2):
                            last = nc.scalar.activation(p[:, j, :], p[:, j, :], ACT_F.Exp, bias=mx[:, i % 2, j:j + 1],
                                                        accum_out=mx[:, 2 + i % 2, j:j + 1])
                        last.then_inc(act_done, 1)
                    c.act += 1
                    prob_m[i] = c.act

                def normalise(i):
                    p = pr[i % 2]
                    if DVE:
                        DVE.wait_ge(act_done, prob_m[i])
                        link(nc.vector.reciprocal(mx[:, 2 + i % 2, :], mx[:, 2 + i % 2, :]))
                        nc.vector.tensor_tensor(p, p, mx[:, 2 + i % 2, :].unsqueeze(2).to_broadcast([P, 2, S]),
                                                ALU.mult).then_inc(dve_done, 1)
                    c.dve += 1
                    b = 2 + i % 2
                    take(b)
                    if PE:
                        PE.wait_ge(dve_done, c.dve)
                        for j in range(2):
                            for k in range(2):
                                last = nc.tensor.transpose(bank[b][:, (2 * j + k) * P:(2 * j + k + 1) * P],
                                                           p[:, j, k * P:(k + 1) * P], ident)
                        last.then_inc(pe_done, 1)
                    c.pe += 1
                    turned_m[i] = c.pe
                    if ACT:
                        if i >= 2:
                            ACT.wait_ge(pe_done, outs_m[i - 2])
                        ACT.wait_ge(pe_done, turned_m[i])
                        nc.scalar.activation(pT[i % 2], bank[b][:, :], ACT_F.Copy).then_inc(act_done, 1)
                    c.act += 1
                    copied_m[i] = c.act
                    bank_free[b] = ("act", c.act)

                def weigh(i):
                    br, m, u = units[i]
                    base, heads = same_half(u)
                    b = 4 + i % 2
                    take(b)
                    if PE:
                        PE.wait_ge(act_done, copied_m[i])
                        for j, h in enumerate(heads):
                            for k in range(2):
                                v = (z[:, k, Z_VA + HD * h:Z_VA + HD * (h + 1)] if br == 0
                                     else kv[:, k, P * h + HD:P * (h + 1)])
                                last = nc.tensor.matmul(bank[b][base:base + HD, j * P:(j + 1) * P], v,
                                                        pT[i % 2][:, (2 * j + k) * P:(2 * j + k + 1) * P],
                                                        start=(k == 0), stop=(k == 1))
                        last.then_inc(pe_done, 1)
                    c.pe += 1
                    outs_m[i] = c.pe
                    read_out(b, fn_act=lambda: nc.scalar.activation(
                        yT[br][base:base + HD, heads[0] // 2:heads[0] // 2 + 2, m * P:(m + 1) * P],
                        bank[b][base:base + HD, 0:2 * P].rearrange("p (a b) -> p a b", a=2), ACT_F.Copy))

                parts = chain(*(modulation(s) for s in slabs))
                logits(0)
                for i in range(len(units) + 2):
                    if i + 1 < len(units):
                        logits(i + 1)
                        next(parts)
                    if i < len(units):
                        softmax(i)
                    if 1 <= i <= len(units):
                        normalise(i - 1)
                    if i >= 2:
                        weigh(i - 2)
                for _ in parts:
                    pass
                merged = work.rearrange("p (m d) -> p m d", m=TT)

                def gated(which):
                    def read(m, s, h0, n, b):
                        def fn():
                            g = z[:, m, (Z_GA, Z_GB)[which] + h0:(Z_GA, Z_GB)[which] + h0 + n]
                            if which == 0:
                                return nc.vector.tensor_tensor(merged[:, m, h0:h0 + n], bank[b][:, 0:n], g, ALU.mult)
                            link(nc.vector.tensor_tensor(g, bank[b][:, 0:n], g, ALU.mult))
                            return nc.vector.tensor_tensor(merged[:, m, h0:h0 + n], merged[:, m, h0:h0 + n], g, ALU.add)
                        read_out(b, fn_dve=fn)
                    return read

                if DVE:
                    settle(DVE)
                for br in range(2):
                    rows_product(lambda k, m: yT[br][:, k, m * P:(m + 1) * P], 4, range(TT), [1024], gated(br))
                transposes([(lambda m, k=k: merged[:, m, k * P:(k + 1) * P], hT[:, k, :], P, None, None)
                            for k in range(KD)])
                add_x = lambda m, s, h0, n, b: read_out(b, fn_dve=lambda: nc.vector.tensor_tensor(
                    x[:, m, 512 * s:512 * s + n], x[:, m, 512 * s:512 * s + n], bank[b][:, 0:n], ALU.add))
                rows_product(lambda k, m: hT[:, k, m * P:(m + 1) * P], KD, range(TT), [512, 512], add_x)

                norm_rows(x, xn, TT)
                transposes([(lambda m, k=k: xn[:, m, k * P:(k + 1) * P], hT[:, k, :], P, col(f"ffn{l}", 1, k), None)
                            for k in range(KD)])
                if PE:
                    settle(PE)
                if ACT:
                    settle(ACT)
                cv = [work[:, 512 * i:512 * i + 512].rearrange("p (h s) -> p h s", h=2) for i in range(4)]
                used = {}
                for i in range(FT):
                    if i % 2 == 0:
                        w = open_slab()
                    b = turn()
                    take(b)
                    if PE:
                        for j in range(2):
                            for k in range(KD):
                                at = ((2 * (i % 2) + j) * KD + k) * P
                                last = nc.tensor.matmul(bank[b][:, j * S:(j + 1) * S], w[:, at:at + P], hT[:, k, :],
                                                        start=(k == 0), stop=(k == KD - 1))
                        last.then_inc(pe_done, 1)
                    c.pe += 1
                    if i % 2 == 1:
                        close_slab()
                    o = cv[i % 4]
                    tap = lambda r, j: col(f"conv{l}", 1, r * 2 * FT + j * FT + i)
                    if ACT:
                        ACT.wait_ge(pe_done, c.pe)
                        if i >= 4:
                            ACT.wait_ge(dve_done, used[i - 4])
                        for j in range(2):
                            last = nc.scalar.activation(o[:, j, :], bank[b][:, j * S:(j + 1) * S], ACT_F.Identity,
                                                        scale=tap(2, j), bias=tap(3, j))
                        last.then_inc(act_done, 1)
                    c.act += 1
                    if DVE:
                        DVE.wait_ge(act_done, c.act)
                        for r in range(2):
                            sh = 2 - r
                            for j in (1, 0):
                                last = nc.vector.scalar_tensor_tensor(
                                    o[:, j, sh:S], bank[b][:, j * S:(j + 1) * S - sh], tap(r, j), o[:, j, sh:S],
                                    ALU.mult, ALU.add)
                            if r == 0:
                                link(last)
                        last.then_inc(dve_done, 1)
                    c.dve += 1
                    bank_free[b] = ("dve", c.dve)
                    if ACT:
                        ACT.wait_ge(dve_done, c.dve)
                        nc.scalar.activation(o[:, 1, :], o[:, 1, :], ACT_F.Silu).then_inc(act_done, 1)
                    c.act += 1
                    if DVE:
                        DVE.wait_ge(act_done, c.act)
                        nc.vector.tensor_tensor(hid[:, i, :], o[:, 0, :], o[:, 1, :], ALU.mult).then_inc(dve_done, 1)
                    c.dve += 1
                    used[i] = c.dve
                if PE:
                    settle(PE)
                for b in range(4):
                    take(b)
                for t in range(FT):
                    if t % 4 == 0:
                        w = open_slab()
                    if PE:
                        for m in range(TT):
                            for h in range(2):
                                last = nc.tensor.matmul(bank[2 * m + h][:, :], hid[:, t, m * P:(m + 1) * P],
                                                        w[:, (t % 4) * D + h * 512:(t % 4) * D + h * 512 + 512],
                                                        start=(t == 0), stop=(t == FT - 1))
                        if t % 4 == 3 or t == FT - 1:
                            last.then_inc(pe_done, 1)
                    if t % 4 == 3 or t == FT - 1:
                        c.pe += 1
                        close_slab()
                for b in range(4):
                    m, h = divmod(b, 2)
                    read_out(b, fn_dve=lambda: nc.vector.tensor_tensor(
                        x[:, m, 512 * h:512 * h + 512], x[:, m, 512 * h:512 * h + 512], bank[b][:, :], ALU.add))

            get = Carve(arena)
            kc2 = get(K2["all"])
            uT = get(KD, T2 * P)
            lora_sb = get(3, 512)
            gain = get(KD, 2)
            ybT = get(4, S)
            keep = get.at
            load(kc2, k2)
            load(lora_sb, lora.rearrange("p (a b) -> p a b", a=3))

            def k2c(name, n=P, at=0):
                return kc2[:, K2[name] + at:K2[name] + at + n]

            def set_gain(g, at):
                if DVE:
                    settle(DVE)
                    link(nc.vector.tensor_scalar(gain, mod[:, at:at + KD, :], 1.0, None, ALU.add))
                    nc.vector.tensor_tensor(gain, gain, g.unsqueeze(2).to_broadcast([P, KD, 2]), ALU.mult)\
                        .then_inc(dve_done, 1)
                c.dve += 1

            ctx_sb = get(TT, D)
            xn = get(TT, D)
            load(ctx_sb, ctx_in.rearrange("b (m p) d -> p (b m) d", p=P))
            set_gain(col("mix2", KD), KD)
            for src, at, which in ((ctx_sb, 0, 1), (x[:, :, :], S, 0)):
                norm_rows(src, xn, TT)
                transposes([(lambda m, k=k: xn[:, m, k * P:(k + 1) * P], uT[:, k, at:at + S], P,
                             gain[:, k, which:which + 1], mod[:, k, which:which + 1]) for k in range(KD)])

            get = Carve(arena, keep)
            bc = get(T2, B_COLS)
            nrow = ROW["a_log"]
            rw = get(nrow)
            roff = 2 * DEPTH * D
            load(rw, rows[0:1, roff:roff + nrow].to_broadcast([P, nrow]))

            def row(name, n=512, at=0):
                return rw[:, ROW[name] + at:ROW[name] + at + n]

            work_at = get.at
            uC = get(KD, S)
            if DVE:
                settle(DVE)
                for k in range(KD):
                    last = nc.vector.tensor_copy(uC[:, k, :].rearrange("p (w r) -> p w r", w=64),
                                                 uT[:, k, S:2 * S].rearrange("p (r w) -> p w r", w=64))
                last.then_inc(dve_done, 1)
            c.dve += 1

            def left_b(k, T):
                if T < 2:
                    return uT[:, k, T * P:(T + 1) * P]
                return uC[:, k, (T - 2) * P:(T - 1) * P]

            rows_product(left_b, KD, range(T2), [512, 512, 512, 384],
                         lambda m, s, h0, n, b: copy_out(b, bc[:, m, 512 * s:512 * s + n], bank[b][:, 0:n]))
            if PE:
                settle(PE)
            for q in range(4):
                cs = slice(480 * q, 480 * q + 480)
                for seq in range(2):
                    bs = []
                    for i in range(2):
                        b = turn()
                        bs.append(b)
                        take(b)
                        if PE:
                            nc.tensor.matmul(bank[b][:, 0:480], k2c("shift"), bc[:, 2 * seq + i, cs], start=True, stop=False)
                            nc.tensor.matmul(bank[b][:, 0:480], k2c("shift_n" if i == 0 else "shift_p"),
                                             bc[:, 2 * seq + 1 - i, cs], start=False, stop=True).then_inc(pe_done, 1)
                        c.pe += 1
                    for i in range(2):
                        b = bs[i]

                        def fn():
                            tmp = arena[:, work_at + 512 * i:work_at + 512 * i + 480]
                            link(nc.vector.tensor_tensor(tmp, bank[b][:, 0:480], row("mu", 480, 480 * q), ALU.mult))
                            return nc.vector.tensor_tensor(bc[:, 2 * seq + i, cs], bc[:, 2 * seq + i, cs], tmp, ALU.add)
                        read_out(b, fn_dve=fn)
            get = Carve(arena, work_at)
            loT = kc[:, P:P + T2 * 2 * P].rearrange("p (a b c) -> p a b c", a=T2, b=2)
            gT = cc[:, 0:TT * P].rearrange("p (a b) -> p a b", a=TT)
            lw, ic, kk, rr = [get(512) for _ in range(4)]
            kds, bbs = [get(512)], [get(512), get(512)]
            aavs = [get(2, RH, CH), ybT.rearrange("p a b -> p (a b)").rearrange("p (a b c) -> p a b c", a=2, b=RH)]
            N0, state = get(2, 4, CH), get(2, 4, CH)
            alt = Carve(uT.rearrange("p a b -> p (a b)"))
            Ms, Mts, Xts, Ys, rbs, rks = [[get(4, P), alt(4, P)] for _ in range(6)]
            wzs = [get(4, 2, CH), alt(4, 2, CH)]
            kds.append(alt(512))
            small = Carve(arena, work_at - nrow + ROW["mu"])
            y, bonus, dcols, stat = small(TT, RH, CH), small(TT, RH), [small(4, 4), small(4, 4)], small(4, RH)
            chT0 = get(4, 4, P)
            low_rank_room = [bc[:, T, 1536 + P * j:1664 + P * j] for T in range(T2) for j in range(3)]
            rTs = [chT0[:, 0, :, :], k2c("reset16", T2 * P).rearrange("p (a b) -> p a b", a=4)]
            bTs = [chT0[:, 1, :, :], small(4, P)]
            kTs = [[chT0[:, 2, i, :] for i in range(4)], low_rank_room[0:4]]
            aTs = [[chT0[:, 3, i, :] for i in range(4)], low_rank_room[4:8]]
            Rt = lw.rearrange("p (a b) -> p a b", a=4)
            ph = kk.rearrange("p (c a b) -> p c a b", c=2, a=4)
            qs = ic.rearrange("p (c a b) -> p c a b", c=2, a=4)
            flat = lambda a: a.rearrange("p a b -> p (a b)")
            forward = (lw, ic, kk, rr, flat(Ys[0]), flat(Ms[0]), flat(Mts[0]), stat[:, 0, :])
            backward = tuple(flat(a[i]) for a, i in ((Xts, 0), (rbs, 0), (rks, 0), (Ys, 1), (Ms, 1), (Mts, 1), (Xts, 1)))
            backward += (stat[:, 1, :],)
            heads = lambda a: a.rearrange("p (h d) -> p h d", d=CH)
            if SP:
                settle(SP)
                SP.dma_start(u_dram, uT).then_inc(spilled, 16)
                SP.wait_ge(spilled, 16)
                SP.dma_start(ss[0:1, 63:64], rw[0:1, 0:1]).then_inc(loaded, 16)
            c.sp += 1
            if POOL:
                settle(POOL)
                nc.gpsimd.memset(state.rearrange("p a b c -> p (a b c)"), 0.0).then_inc(pool_done, 1)
            c.pool += 1
            if ACT:
                settle(ACT)
                nc.scalar.activation(bc[:, :, 1536:1664], bc[:, :, 1536:1664], ACT_F.Tanh)
                nc.scalar.activation(bc[:, :, 1792:1920], bc[:, :, 1792:1920], ACT_F.Sigmoid).then_inc(act_done, 1)
            c.act += 1
            transposes([(lambda m, T=T, j=j: bc[:, T, 1536 + P * j:1664 + P * j], loT[:, T, j, :], P, None, None)
                        for T in range(T2) for j in range(2)]
                       + [(lambda m, T=T: bc[:, 2 + T, 1792:1920], gT[:, T, :], P, None, None) for T in range(TT)], tiles=1)

            def dve_step(fn):
                if DVE:
                    settle(DVE)
                    fn().then_inc(dve_done, 1)
                c.dve += 1

            def act_step(fn):
                if ACT:
                    settle(ACT)
                    fn().then_inc(act_done, 1)
                c.act += 1

            def pe_step(b, fn):
                if PE:
                    settle(PE)
                    fn(bank[b]).then_inc(pe_done, 1)
                c.pe += 1

            tt = nc.vector.tensor_tensor
            mm = nc.tensor.matmul
            all4 = lambda a: a.unsqueeze(1).to_broadcast([P, 4, P])
            b4 = lambda b: bank[b][:, :].rearrange("p (a b) -> p a b", a=4)

            def each4(f, n=P):
                def fn(bk):
                    for i in range(4):
                        last = f(bk[:, n * i:n * i + n], i)
                    return last
                return fn

            class Stream:

                def __init__(self, banks, heads=2):
                    self.banks, self.pe, self.fresh = banks, 0, True
                    self.marks = {"dve": 0, "act": 0}
                    self.n, self.per = heads, 4 // heads
                    self.far = self.per * (len(banks) // 2)

                def slot(self, k, rows_=slice(0, P), wide=1):
                    at, n = self.n * P * (k % self.per), self.n
                    return bank[self.banks[k // self.per]][rows_, at:at + n * wide * P]\
                        .rearrange("p (a b) -> p a b", a=n)

                def step(self, name, fn, alone=True):
                    eng = {"pe": PE, "dve": DVE, "act": ACT}[name]
                    if eng:
                        if self.fresh:
                            settle(eng)
                        elif name == "pe":
                            for other in ("dve", "act"):
                                if self.marks[other]:
                                    eng.wait_ge(done[other], self.marks[other])
                        else:
                            if self.pe:
                                eng.wait_ge(pe_done, self.pe)
                            for other in ("dve", "act"):
                                if alone and self.marks[other]:
                                    eng.wait_ge(done[other], self.marks[other])
                        fn().then_inc(done[name], 1)
                    self.fresh = False
                    if name == "pe":
                        c.pe += 1
                    elif name == "dve":
                        c.dve += 1
                    else:
                        c.act += 1
                    if name == "pe":
                        self.pe = c.pe
                    else:
                        self.marks[name] = c.of(name)

            def side_by_side(chains):
                for _ in zip_longest(*chains):
                    pass

            all2 = lambda a, n=2: a.unsqueeze(1).to_broadcast([P, n, P])

            def invert(S, d, X, Mt, Xt, Y):
                for level in range(1, LEVELS):
                    def residual():
                        for i in range(S.n):
                            last = mm(S.slot(0)[:, i, :], Mt[:, i, :], X[:, i, :], start=True, stop=True)
                        return last
                    S.step("pe", residual)
                    S.step("dve", lambda: tt(Y, S.slot(0), all2(k2c(f"level{d}", P, P * level), S.n), ALU.mult))
                    yield

                    def refine():
                        for i in range(S.n):
                            last = mm(S.slot(S.far)[:, i, :], Y[:, i, :], Xt[:, i, :], start=True, stop=True)
                        if level < LEVELS - 1:
                            for i in range(S.n):
                                last = mm(S.slot(0)[:, i, :], Xt[:, i, :], Y[:, i, :], start=True, stop=True)
                        return last
                    S.step("pe", refine)
                    if level < LEVELS - 1:
                        S.step("act", lambda: nc.scalar.activation(X, S.slot(0), ACT_F.Copy))
                    S.step("dve", lambda: nc.vector.tensor_copy(Xt, S.slot(S.far)), alone=False)
                    yield

            def heads_chain(S, g, half, seq, step, d, T):
                v = bc[:, T, 1024:1536]
                rT, bT, kT, aT = rTs[d], bTs[d], kTs[d], aTs[d]
                block = lambda a, i: a[i][ch, :] if isinstance(a, list) else a[ch, i, :]
                kd, bb, aav, dcol = kds[d], bbs[d], aavs[d], dcols[d]
                ch = slice(CH * g, CH * g + CH)
                two = slice(2 * half, 2 * half + 2)
                idx = [2 * half, 2 * half + 1]
                hs = [2 * i + g for i in idx]
                M, Mt, Xt, Y, rb, rk = [a[g][:, two, :] for a in (Ms, Mts, Xts, Ys, rbs, rks)]
                wz = wzs[g][:, two, :, :]
                ak = Y
                tok = lambda a, i: a[:, CH * hs[i]:CH * hs[i] + CH]

                def products():
                    for k, (p_, q_) in enumerate(((aT, bT), (bT, aT), (kT, aT), (bT, rT))):
                        for i in range(2):
                            last = mm(S.slot(k)[:, i, :], block(p_, idx[i]), block(q_, idx[i]), start=True, stop=True)
                    return last
                S.step("pe", products)

                def masks():
                    tt(M, S.slot(0), all2(k2c(f"nstrict{d}")), ALU.mult)
                    tt(Mt, S.slot(1), all2(k2c(f"nstrictT{d}")), ALU.mult)
                    tt(ak, S.slot(2), all2(k2c(f"strictT{d}")), ALU.mult)
                    link(tt(rb, S.slot(3), all2(k2c(f"inclT{d}")), ALU.mult))
                    tt(M, M, all2(ident), ALU.add)
                    link(tt(Mt, Mt, all2(ident), ALU.add))
                    tt(Xt, Mt, all2(k2c(f"level{1 - d}")), ALU.mult)
                    return tt(M, M, all2(k2c(f"level{d}")), ALU.mult)
                S.step("dve", masks)
                yield

                def products2():
                    for i in range(2):
                        mm(S.slot(0)[:, i, :], block(kT, idx[i]), rT[ch, idx[i], :], start=True, stop=True)
                    for i in range(2):
                        last = mm(S.slot(2)[:, i, 0:CH], ak[:, i, :], tok(v, i), start=True, stop=True)
                    return last
                S.step("pe", products2)
                av = aav[:, 1, :, :].rearrange("p (i g) c -> p i g c", g=2)[:, two, g, :]
                S.step("act", lambda: nc.scalar.activation(av, S.slot(2)[:, :, 0:CH], ACT_F.Copy))
                S.step("dve", lambda: tt(rk, S.slot(0), all2(k2c(f"inclT{d}")), ALU.mult), alone=False)
                yield
                yield from invert(S, d, M, Mt, Xt, Y)

                def solve():
                    for i in range(2):
                        last = mm(S.slot(0)[:, i, :], Xt[:, i, :], aav[:, :, hs[i], :], start=True, stop=True)
                    return last
                S.step("pe", solve)
                S.step("act", lambda: nc.scalar.activation(
                    wz, S.slot(0).rearrange("p a (w c) -> p a w c", w=2), ACT_F.Copy))
                yield

                def parts_products():
                    for i in range(2):
                        mm(S.slot(0, ch)[:, i, :], wz[:, i, 0, :], rb[:, i, :], start=True, stop=True)
                    for cc_ in range(2):
                        tk = slice(CH * cc_, CH * cc_ + CH)
                        o = S.slot(1 + cc_, ch)
                        for i in range(2):
                            mm(o[:, i, 0:CH], wz[tk, i, 0, :], tok(bb, i)[tk, :], start=True, stop=True)
                            mm(o[:, i, CH:P], tok(bb, i)[tk, :], wz[tk, i, 1, :], start=True, stop=False)
                            last = mm(o[:, i, CH:P], tok(kd, i)[tk, :], tok(v, i)[tk, :], start=False, stop=True)
                    return last
                S.step("pe", parts_products)

                def parts():
                    tt(Rt[ch, two, :], S.slot(0, ch), rT[ch, two, :], ALU.add)
                    for cc_ in range(2):
                        tt(ph[ch, cc_, two, :], S.slot(1 + cc_, ch)[:, :, 0:CH],
                           ident[ch, ch].unsqueeze(1).to_broadcast([CH, 2, CH]), ALU.add)
                        nc.vector.tensor_copy(qs[ch, cc_, two, :], S.slot(1 + cc_, ch)[:, :, CH:P])
                    return tt(N0[ch, first, two, :], st, scale(first, 0), ALU.mult)
                st = state[ch, d, two, :]
                scale = lambda cc_, j: dcol[ch, two, 2 * cc_ + j:2 * cc_ + j + 1].to_broadcast([CH, 2, CH])
                first = 0 if d == 0 else 1
                S.step("dve", parts)
                yield
                for cc_ in (first, 1 - first):
                    def move():
                        for i in range(2):
                            last = mm(S.slot(3, ch)[:, i, 0:CH], ph[ch, cc_, idx[i], :], N0[ch, cc_, idx[i], :],
                                      start=True, stop=True)
                        return last
                    S.step("pe", move)

                    def update():
                        link(tt(st, S.slot(3, ch)[:, :, 0:CH], qs[ch, cc_, two, :], ALU.add))
                        if cc_ != first:
                            return tt(st, st, scale(cc_, 1), ALU.mult)
                        link(tt(st, st, scale(cc_, 1), ALU.mult))
                        return tt(N0[ch, 1 - cc_, two, :], st, scale(1 - cc_, 0), ALU.mult)
                    S.step("dve", update)
                    yield
                if seq == 1:
                    def outputs():
                        for i in range(2):
                            o = S.slot(0)[:, i, 0:CH]
                            mm(o, rb[:, i, :], wz[:, i, 1, :], start=True, stop=False)
                            mm(o, rk[:, i, :], tok(v, i), start=False, stop=True)
                        for i in range(2):
                            for cc_ in range(2):
                                tk = slice(CH * cc_, CH * cc_ + CH)
                                last = mm(S.slot(2, tk)[:, i, 0:CH], Rt[ch, idx[i], tk], N0[ch, cc_, idx[i], :],
                                          start=True, stop=True)
                        return last
                    S.step("pe", outputs)
                    yv = y[:, T - 2, :, :].rearrange("p (i g) c -> p i g c", g=2)[:, two, g, :]

                    def add_y():
                        if step == 0:
                            link(nc.vector.tensor_copy(yv, S.slot(0)[:, :, 0:CH]))
                        else:
                            link(tt(yv, yv, S.slot(0)[:, :, 0:CH], ALU.add))
                        return tt(yv, yv, S.slot(2)[:, :, 0:CH], ALU.add)
                    S.step("dve", add_y)
                    yield

            def prepare(seq, step, d, T):
                S = Stream((3 * d, 3 * d + 1, 3 * d + 2))
                b0, b1, b2 = [bank[b] for b in S.banks]
                lw, ic, kk, rr, e_p, e_n, e_x, stat = (forward, backward)[d]
                kd, bb, aav, dcol = kds[d], bbs[d], aavs[d], dcols[d]
                r, k, v = [bc[:, T, 512 * i:512 * i + 512] for i in range(3)]
                lo = slice(CH * d, CH * d + CH)
                sums = ss[:, RH * d:RH * d + RH]

                def low_rank():
                    mm(b0[:, :], loT[lo, T, 0, :], lora_sb[lo, 0, :], start=True, stop=True)
                    return mm(b1[:, :], loT[lo, T, 1, :], lora_sb[lo, 1, :], start=True, stop=True)
                S.step("pe", low_rank)

                def pre():
                    tt(lw, b0[:, :], row("w0", 512, 512 * d), ALU.add)
                    tt(kk, k, row("k_k"), ALU.mult)
                    return tt(ic, b1[:, :], row("a0", 512, 512 * d), ALU.add)
                S.step("dve", pre)
                yield

                def sig():
                    nc.scalar.activation(ic, ic, ACT_F.Sigmoid)
                    return nc.scalar.activation(lw, lw, ACT_F.Sigmoid)
                S.step("act", sig)

                def squares():
                    link(tt(heads(rr), heads(kk), heads(kk), ALU.mult))
                    link(nc.vector.tensor_reduce(sums, heads(rr), AX, ALU.add))
                    return nc.vector.tensor_scalar(sums, sums, 1.0, EPS, ALU.mult, ALU.add)
                S.step("dve", squares)
                S.step("act", lambda: nc.scalar.activation(sums, sums, ACT_F.Sqrt))
                yield

                def keys():
                    link(nc.vector.reciprocal(sums, sums))
                    link(tt(heads(kk), heads(kk), sums.unsqueeze(2).to_broadcast([P, RH, CH]), ALU.mult))
                    nc.vector.tensor_scalar(lw, lw, -math.exp(-0.5), None, ALU.mult)
                    tt(bb, kk, ic, ALU.mult)
                    link(nc.vector.scalar_tensor_tensor(kd, ic, -1.0, row("k_a"), ALU.add, ALU.mult))
                    return nc.vector.scalar_tensor_tensor(kd, kd, 1.0, k, ALU.add, ALU.mult)
                S.step("dve", keys)

                def running():
                    mm(b0[:, :], k2c(f"cum{d}"), lw, start=True, stop=True)
                    mm(b1[:, :], k2c(f"cumx{d}"), lw, start=True, stop=True)
                    return each4(lambda o, i: mm(o, lw[:, P * i:P * i + P], k2c(f"col4{d}", 4),
                                                 start=True, stop=True), 4)(b2)
                S.step("pe", running)
                yield

                def exps():
                    nc.scalar.activation(e_p, b0[:, :], ACT_F.Exp)
                    nc.scalar.activation(e_n, b0[:, :], ACT_F.Exp, scale=-1.0)
                    nc.scalar.activation(e_x, b1[:, :], ACT_F.Exp)
                    return nc.scalar.activation(dcol, b2[:, 0:16].rearrange("p (a b) -> p a b", a=4), ACT_F.Exp)
                S.step("act", exps)
                if seq == 1:
                    def bonus_fn():
                        link(tt(rr, r, kd, ALU.mult))
                        link(tt(rr, rr, row("r_k"), ALU.mult))
                        if step == 0:
                            return nc.vector.tensor_reduce(bonus[:, T - 2, :], heads(rr), AX, ALU.add)
                        link(nc.vector.tensor_reduce(stat, heads(rr), AX, ALU.add))
                        return tt(bonus[:, T - 2, :], bonus[:, T - 2, :], stat, ALU.add)
                    S.step("dve", bonus_fn, alone=False)
                yield

                def scaled():
                    tt(rr, r, e_p, ALU.mult)
                    tt(kd, kd, e_n, ALU.mult)
                    tt(bb, bb, e_n, ALU.mult)
                    return nc.vector.scalar_tensor_tensor(aav[:, 0, :, :], heads(kk), -1.0, heads(e_x),
                                                          ALU.mult, ALU.mult)
                S.step("dve", scaled)
                yield

            for seq in range(2):
                for step in range(2):
                    tile = lambda d: 2 * seq + (step if d == 0 else 1 - step)
                    side_by_side([prepare(seq, step, d, tile(d)) for d in range(2)])
                    jobs = []
                    for d, r_scaled in enumerate((rr, backward[3])):
                        a_scaled = aavs[d][:, 0, :, :].rearrange("p a b -> p (a b)")
                        for src, dst in ((r_scaled, [rTs[d][:, i, :] for i in range(4)]),
                                         (bbs[d], [bTs[d][:, i, :] for i in range(4)]),
                                         (kds[d], kTs[d]), (a_scaled, aTs[d])):
                            jobs += [(lambda m, src=src, i=i: src[:, P * i:P * i + P], dst[i], P, None, None)
                                     for i in range(4)]
                    transposes(jobs, tiles=1)

                    def both_directions(g, half):
                        S = Stream((4 * g + 2 * half, 4 * g + 2 * half + 1))
                        for d in range(2):
                            yield from heads_chain(S, g, half, seq, step, d, tile(d))
                    side_by_side([both_directions(g, half) for g in range(2) for half in range(2)])
            load(k2c("reset16", T2 * P), k2[:, K2["reset16"]:K2["reset16"] + T2 * P])
            def finish_tile(m):
                S = Stream((m,))
                ym = y[:, m, :, :]
                yf = ym.rearrange("p h c -> p (h c)")
                room = (rr, kk)[m]
                mean, var = stat[:, 2 * m, :], stat[:, 2 * m + 1, :]
                wide = lambda a: a.unsqueeze(2).to_broadcast([P, RH, CH])
                S.step("pe", lambda: mm(bank[m][:, :], gT[:, m, :], lora_sb[:, 2, :], start=True, stop=True))

                def centre():
                    link(nc.vector.tensor_reduce(mean, ym, AX, ALU.add))
                    link(nc.vector.tensor_scalar(mean, mean, 1.0 / CH, None, ALU.mult))
                    link(tt(ym, ym, wide(mean), ALU.subtract))
                    link(tt(heads(room), ym, ym, ALU.mult))
                    link(nc.vector.tensor_reduce(var, heads(room), AX, ALU.add))
                    return nc.vector.tensor_scalar(var, var, 1.0 / CH, 1e-5 * CH, ALU.mult, ALU.add)
                S.step("dve", centre)
                S.step("act", lambda: nc.scalar.activation(var, var, ACT_F.Sqrt))
                yield

                def finish_y():
                    link(nc.vector.reciprocal(var, var))
                    link(tt(ym, ym, wide(var), ALU.mult))
                    link(tt(yf, yf, row("lnx_g"), ALU.mult))
                    link(tt(yf, yf, row("lnx_b"), ALU.add))
                    link(tt(heads(room), heads(bc[:, 2 + m, 1024:1536]), wide(bonus[:, m, :]), ALU.mult))
                    link(tt(yf, yf, room, ALU.add))
                    return tt(yf, yf, bank[m][:, :], ALU.mult)
                S.step("dve", finish_y)
                yield
            side_by_side([finish_tile(m) for m in range(TT)])
            yflat = y.rearrange("p m h c -> p m (h c)")
            transposes([(lambda m, i=i: yflat[:, m, P * i:P * i + P],
                         ybT[:, i, :].rearrange("p (r w) -> p w r", w=64), P, None, None) for i in range(4)])

            load(uT, u_dram)
            get = Carve(arena, keep)
            ntail = ROW["all"] - nrow
            rt_ = get(ntail)
            load(rt_, rows[0:1, roff + nrow:roff + ROW["all"]].to_broadcast([P, ntail]))

            def tail(name, n, at=0):
                o = ROW[name] - nrow + at
                return rt_[:, o:o + n]

            yaT = get(4, S)
            zz = get(TT, 512)
            ab = get(T2, 16)
            gt, soft, rest = get(T2, 8), get(T2, 8), get(T2, 8)
            cv = get(12, T2 * P)
            raw_at = get.at
            raw = get(12, 2, S + 4)
            if POOL:
                settle(POOL)
                nc.gpsimd.memset(raw[:, :, :, 0:2], 0.0)
                nc.gpsimd.memset(raw[:, :, :, S + 2:S + 4], 0.0).then_inc(pool_done, 1)
            c.pool += 1
            if PE:
                settle(PE)
            for s in range(3):
                w = open_slab()
                for t in range(4):
                    i = 4 * s + t
                    b = turn()
                    take(b)
                    if PE:
                        for k in range(KD):
                            last = mm(bank[b][:, :], w[:, (t * KD + k) * P:(t * KD + k + 1) * P], uT[:, k, :],
                                      start=(k == 0), stop=(k == KD - 1))
                        last.then_inc(pe_done, 1)
                    c.pe += 1
                    read_out(b, fn_act=lambda: nc.scalar.activation(
                        raw[:, i, :, 2:S + 2], bank[b][:, :].rearrange("p (a b) -> p a b", a=2), ACT_F.Copy))
                    if DVE:
                        DVE.wait_ge(act_done, c.act)
                        if i == 0:
                            DVE.wait_ge(pool_done, c.pool)
                        o = cv[:, i, :].rearrange("p (a b) -> p a b", a=2)
                        tap = lambda j: col("gconv", 1, 12 * j + i)
                        link(nc.vector.tensor_scalar(o, raw[:, i, :, 0:S], tap(0), None, ALU.mult))
                        for j in range(1, 5):
                            last = nc.vector.scalar_tensor_tensor(o, raw[:, i, :, j:S + j], tap(j), o, ALU.mult, ALU.add)
                            if j < 4:
                                link(last)
                        last.then_inc(dve_done, 1)
                    c.dve += 1
                close_slab()
            act_step(lambda: nc.scalar.activation(cv, cv, ACT_F.Silu))
            rows_product(lambda k, m: uT[:, k, S + m * P:S + (m + 1) * P], KD, range(TT), [512],
                         lambda m, s, h0, n, b: copy_out(b, zz[:, m, :], bank[b][:, :]))
            rows_product(lambda k, m: uT[:, k, m * P:(m + 1) * P], KD, range(T2), [16],
                         lambda m, s, h0, n, b: copy_out(b, ab[:, m, :], bank[b][:, 0:16]))
            squares = Carve(arena, raw_at)(4, 2, T2 * P)

            def unit_length(j):
                S = Stream((j,))
                bk, sq, rs = bank[j], squares[:, j, 0, :], squares[:, j, 1, :]
                for i in (j, j + 4):
                    S.step("act", lambda: nc.scalar.activation(sq, cv[:, i, :], ACT_F.Square))
                    S.step("pe", lambda: mm(bk[:, :], k2c("ones"), sq, start=True, stop=True))
                    yield
                    S.step("dve", lambda: nc.vector.tensor_scalar(rs, bk[:, :], EPS, None, ALU.add))
                    S.step("act", lambda: nc.scalar.activation(rs, rs, ACT_F.Sqrt))
                    yield

                    def unit():
                        link(nc.vector.reciprocal(rs, rs))
                        if i >= 4:
                            return tt(cv[:, i, :], cv[:, i, :], rs, ALU.mult)
                        return nc.vector.scalar_tensor_tensor(cv[:, i, :], cv[:, i, :], P ** -0.5, rs,
                                                              ALU.mult, ALU.mult)
                    S.step("dve", unit)
                    yield
            side_by_side([unit_length(j) for j in range(4)])
            bt = ab[:, :, 8:16]
            wide8 = lambda n: tail(n, 8).unsqueeze(1).to_broadcast([P, T2, 8])
            dve_step(lambda: tt(gt, ab[:, :, 0:8], wide8("dt"), ALU.add))

            def softplus_exp():
                link(nc.scalar.activation(soft, gt, ACT_F.Abs))
                nc.scalar.activation(bt, bt, ACT_F.Sigmoid)
                nc.scalar.activation(tail("a_log", 8), tail("a_log", 8), ACT_F.Exp)
                return nc.scalar.activation(soft, soft, ACT_F.Exp, scale=-1.0)
            act_step(softplus_exp)
            lg = ab[:, :, 0:8]

            def log1p():
                link(nc.vector.tensor_scalar(rest, soft, 2.0, None, ALU.add))
                link(nc.vector.reciprocal(rest, rest))
                link(tt(soft, soft, rest, ALU.mult))
                link(tt(rest, soft, soft, ALU.mult))
                link(nc.vector.tensor_scalar(lg, rest, 1.0 / 17, None, ALU.mult))
                for n in (15, 13, 11, 9, 7, 5, 3):
                    link(nc.vector.scalar_tensor_tensor(lg, lg, 1.0 / n, rest, ALU.add, ALU.mult))
                link(nc.vector.scalar_tensor_tensor(lg, lg, 1.0, soft, ALU.add, ALU.mult))
                link(nc.vector.tensor_scalar(lg, lg, 2.0, None, ALU.mult))
                link(nc.vector.scalar_tensor_tensor(gt, gt, 0.0, lg, ALU.max, ALU.add))
                return nc.vector.scalar_tensor_tensor(gt, gt, -1.0, wide8("a_log"), ALU.mult, ALU.mult)
            dve_step(log1p)

            get = Carve(arena, raw_at)
            kt, kd_, qe, kb_, Dm, DT, M, Mt, Xt, Y, QK, qeT, kbT, Qt = [get(4, P) for _ in range(14)]
            rhs, uw = get(4, 2, P), get(4, 2, P)
            Ph, sc2, ku = get(2, 4, P), get(2, 4, P), get(2, 4, P)
            st2 = get(2, 4, P)
            oy = get(TT, 4, P)
            gcr, inc = get(2, T2 * P), get(2, T2 * P // 16)
            gcc, gl, kend = get(T2, 2, 4), get(T2, 2, 4), get(T2, 2, 4)
            gend = get(2 * T2 * 2, 4)
            X = M
            if POOL:
                settle(POOL)
                nc.gpsimd.memset(st2.rearrange("p a b c -> p (a b c)"), 0.0).then_inc(pool_done, 1)
            c.pool += 1
            for d in range(2):
                pe_step(d, lambda bk: [nc.tensor.transpose(bk[0:4, P * T:P * T + P], gt[:, T, 4 * d:4 * d + 4], ident)
                                       for T in range(T2)][-1])
                act_step(lambda: nc.scalar.activation(gcr[0:4, d, :], bank[d][0:4, :], ACT_F.Copy))

            def running():
                n, nb = T2 * P, T2 * P // 16
                reset, reset_b = k2c("reset16", n)[0:4, :], k2c("reset4", nb)[0:4, :]
                for d in range(2):
                    way = slice(None, None, 1 if d == 0 else -1)
                    row_, tot = gcr[0:4, d, :][:, way], inc[0:4, d, :][:, way]
                    link(nc.vector.tensor_tensor_scan(row_, reset, row_, 0.0, ALU.mult, ALU.add))
                    ends = gcr[0:4, d, 15::16] if d == 0 else gcr[0:4, d, 0::16]
                    link(nc.vector.tensor_copy(inc[0:4, d, :], ends))
                    link(nc.vector.tensor_tensor_scan(tot, reset_b, tot, 0.0, ALU.mult, ALU.add))
                    blocks = gcr[0:4, d, :].rearrange("p (c b i) -> p c b i", b=4, i=16)
                    sums_ = inc[0:4, d, :].rearrange("p (c b) -> p c b", b=4)
                    here, prev = (slice(1, 4), slice(0, 3)) if d == 0 else (slice(0, 3), slice(1, 4))
                    for cb in range(T2 * P // CH):
                        last = tt(blocks[:, cb, here, :], blocks[:, cb, here, :],
                                  sums_[:, cb, prev].unsqueeze(2).to_broadcast([4, 3, 16]), ALU.add)
                    link(last)
                return nc.vector.tensor_copy(inc[0:4, 0, 0:1], inc[0:4, 0, 0:1])
            dve_step(running)
            pe_step(0, lambda bk: [nc.tensor.transpose(bk[:, (2 * T + d) * 4:(2 * T + d) * 4 + 4],
                                                       gcr[0:4, d, P * T:P * T + P], ident[0:4, 0:4])
                                   for T in range(T2) for d in range(2)][-1])
            dve_step(lambda: nc.vector.tensor_copy(gcc.rearrange("p a b c -> p (a b c)"), bank[0][:, 0:32]))

            def ends_fn(bk):
                for T in range(T2):
                    for d in range(2):
                        mm(bk[:, (2 * T + d) * 4:(2 * T + d) * 4 + 4], k2c(f"last{d}"), gcc[:, T, d, :], start=True, stop=True)
                        for cc_ in range(2):
                            at = CH * cc_ + (CH - 1 if d == 0 else 0)
                            o = 64 + ((2 * T + d) * 2 + cc_) * 4
                            last = mm(bk[:, o:o + 4], ident[:, at:at + 1].to_broadcast([P, P]), gcc[:, T, d, :],
                                      start=True, stop=True)
                return last
            pe_step(1, ends_fn)
            dve_step(lambda: tt(kend.rearrange("p a b c -> p (a b c)"), bank[1][:, 0:32],
                                gcc.rearrange("p a b c -> p (a b c)"), ALU.subtract))

            def exps3():
                nc.scalar.activation(gl.rearrange("p a b c -> p (a b c)"), gcc.rearrange("p a b c -> p (a b c)"), ACT_F.Exp)
                nc.scalar.activation(kend, kend, ACT_F.Exp)
                return nc.scalar.activation(gend.rearrange("p a b -> p (a b)"), bank[1][:, 64:128], ACT_F.Exp)
            act_step(exps3)

            def delta_chain(h0, n, banks):
                S = Stream(banks, n)
                hs = list(range(h0, h0 + n))
                hh = slice(h0, h0 + n)
                kt_, kdh, qeh, kbh, Dh, DTh, Mh, Mth, Xth, Yh, QKh, qeTh, kbTh, Qth = [
                    a[:, hh, :] for a in (kt, kd_, qe, kb_, Dm, DT, M, Mt, Xt, Y, QK, qeT, kbT, Qt)]
                rhsh, uwh = rhs[:, hh, :, :], uw[:, hh, :, :]
                wide = lambda a: a.unsqueeze(2).to_broadcast([P, n, P])
                alln = lambda a: all2(a, n)

                def each(slot, f):
                    for i in range(n):
                        last = f(S.slot(slot)[:, i, :], i)
                    return last

                for seq in range(2):
                    for step in range(2):
                        for d in range(2):
                            T = 2 * seq + (step if d == 0 else 1 - step)
                            tk = slice(P * T, P * T + P)
                            beta, egc, ken = [a[:, hh] for a in (bt[:, T, 4 * d:4 * d + 4], gl[:, T, d, :], kend[:, T, d, :])]
                            st = st2[:, d, hh, :]
                            first = 0 if d == 0 else 1

                            def turned():
                                each(0, lambda o, i: mm(o, ident[0:4, hs[i]:hs[i] + 1].to_broadcast([4, P]), gcr[0:4, d, tk],
                                                        start=True, stop=True))
                                each(1, lambda o, i: nc.tensor.transpose(o, cv[:, 4 + hs[i], tk], ident))
                                each(2, lambda o, i: nc.tensor.transpose(o, cv[:, 8 + hs[i], tk], ident))
                                return each(3, lambda o, i: nc.tensor.transpose(o, cv[:, hs[i], tk], ident))
                            S.step("pe", turned)

                            def decay():
                                for i in range(n):
                                    r_, g_ = S.slot(0)[:, i, :], gcc[:, T, d, hs[i]:hs[i] + 1]
                                    nc.vector.scalar_tensor_tensor(Dh[:, i, :], r_, g_, k2c(f"nstrict{d}"), ALU.subtract, ALU.mult)
                                    last = nc.vector.scalar_tensor_tensor(DTh[:, i, :], r_, g_, k2c(f"inclT{d}"),
                                                                          ALU.subtract, ALU.mult)
                                return last
                            S.step("dve", decay)

                            def exps2():
                                nc.scalar.activation(Dh, Dh, ACT_F.Exp)
                                return nc.scalar.activation(DTh, DTh, ACT_F.Exp)
                            S.step("act", exps2)

                            def prep():
                                link(nc.vector.tensor_copy(kt_, S.slot(1)))
                                tt(rhsh[:, :, 1, :], S.slot(2), wide(beta), ALU.mult)
                                tt(qeh, S.slot(3), wide(egc), ALU.mult)
                                link(tt(kbh, kt_, wide(beta), ALU.mult))
                                tt(kdh, kt_, wide(ken), ALU.mult)
                                return tt(rhsh[:, :, 0, :], kbh, wide(egc), ALU.mult)
                            S.step("dve", prep, alone=False)
                            yield

                            def turned2():
                                each(4, lambda o, i: nc.tensor.transpose(o, kbh[:, i, :], ident))
                                return each(5, lambda o, i: nc.tensor.transpose(o, qeh[:, i, :], ident))
                            S.step("pe", turned2)

                            def keep2():
                                nc.scalar.activation(kbTh, S.slot(4), ACT_F.Copy)
                                return nc.scalar.activation(qeTh, S.slot(5), ACT_F.Copy)
                            S.step("act", keep2)
                            yield

                            def products3():
                                each(0, lambda o, i: mm(o, kbTh[:, i, :], cv[:, 4 + hs[i], tk], start=True, stop=True))
                                each(1, lambda o, i: mm(o, cv[:, 4 + hs[i], tk], kbTh[:, i, :], start=True, stop=True))
                                return each(2, lambda o, i: mm(o, cv[:, 4 + hs[i], tk], cv[:, hs[i], tk], start=True, stop=True))
                            S.step("pe", products3)

                            def masks2():
                                tt(Mh, S.slot(0), Dh, ALU.mult)
                                tt(Mth, S.slot(1), DTh, ALU.mult)
                                link(tt(QKh, S.slot(2), DTh, ALU.mult))
                                tt(Mh, Mh, alln(k2c(f"nstrict{d}")), ALU.mult)
                                tt(Mth, Mth, alln(k2c(f"strictT{d}")), ALU.mult)
                                link(tt(QKh, QKh, alln(k2c(f"inclT{d}")), ALU.mult))
                                tt(Mh, alln(ident), Mh, ALU.subtract)
                                link(tt(Mth, Mth, alln(ident), ALU.add))
                                tt(Xth, Mth, alln(k2c(f"level{1 - d}")), ALU.mult)
                                return tt(Mh, Mh, alln(k2c(f"level{d}")), ALU.mult)
                            S.step("dve", masks2)
                            yield
                            yield from invert(S, d, Mh, Mth, Xth, Yh)
                            two_wide = S.slot(0, wide=2).rearrange("p a (w c) -> p a w c", w=2)

                            def solve():
                                for i in range(n):
                                    last = mm(two_wide[:, i, :, :].rearrange("p a b -> p (a b)"), Xth[:, i, :],
                                              rhsh[:, i, :, :].rearrange("p a b -> p (a b)"), start=True, stop=True)
                                return last
                            S.step("pe", solve)
                            S.step("act", lambda: nc.scalar.activation(uwh, two_wide, ACT_F.Copy))
                            yield
                            last_slot = 2 if n == 1 else 3

                            def parts_products():
                                for cc_ in range(2):
                                    ck = slice(CH * cc_, CH * cc_ + CH)
                                    each(S.far * cc_, lambda o, i: mm(o, uwh[ck, i, 0, :], kdh[ck, i, :], start=True, stop=True))
                                    each(S.far * cc_ + 1, lambda o, i: mm(o, kdh[ck, i, :], uwh[ck, i, 1, :],
                                                                          start=True, stop=True))
                                return each(last_slot, lambda o, i: mm(o, uwh[:, i, 0, :], QKh[:, i, :], start=True, stop=True))
                            S.step("pe", parts_products)

                            def parts():
                                tt(Qth, qeTh, S.slot(last_slot), ALU.subtract)
                                for cc_ in range(2):
                                    for i in range(n):
                                        ge = gend[:, (2 * T + d) * 2 + cc_, hs[i]:hs[i] + 1]
                                        nc.vector.scalar_tensor_tensor(Ph[:, cc_, hs[i], :], ident, ge,
                                                                       S.slot(S.far * cc_)[:, i, :], ALU.mult, ALU.subtract)
                                    nc.vector.tensor_copy(ku[:, cc_, hh, :], S.slot(S.far * cc_ + 1))
                                return nc.vector.tensor_copy(sc2[:, first, hh, :], st)
                            S.step("dve", parts)
                            yield
                            for cc_ in (first, 1 - first):
                                S.step("pe", lambda: each(7, lambda o, i: mm(o, Ph[:, cc_, hs[i], :], st[:, i, :],
                                                                             start=True, stop=True)))

                                def update():
                                    if cc_ != first:
                                        return tt(st, S.slot(7), ku[:, cc_, hh, :], ALU.add)
                                    link(tt(st, S.slot(7), ku[:, cc_, hh, :], ALU.add))
                                    return nc.vector.tensor_copy(sc2[:, 1 - cc_, hh, :], st)
                                S.step("dve", update)
                                yield
                            if seq == 1:
                                def outputs():
                                    for i in range(n):
                                        for cc_ in range(2):
                                            tr = slice(CH * cc_, CH * cc_ + CH)
                                            mm(S.slot(0, tr)[:, i, :], Qth[:, i, tr], sc2[:, cc_, hs[i], :], start=True, stop=True)
                                    return each(4, lambda o, i: mm(o, QKh[:, i, :], uwh[:, i, 1, :], start=True, stop=True))
                                S.step("pe", outputs)

                                def add_o():
                                    o_ = oy[:, T - 2, hh, :]
                                    if step == 0:
                                        link(nc.vector.tensor_copy(o_, S.slot(0)))
                                    else:
                                        link(tt(o_, o_, S.slot(0), ALU.add))
                                    return tt(o_, o_, S.slot(4), ALU.add)
                                S.step("dve", add_o)
                                yield

            side_by_side([delta_chain(*a) for a in DELTA_CHAINS])
            act_step(lambda: nc.scalar.activation(zz, zz, ACT_F.Silu))
            for m in range(TT):
                norm_heads(oy[:, m, :, :], oy[:, m, :, :], qe, 4, P)

                def gate_o():
                    link(tt(oy[:, m, :, :], oy[:, m, :, :], all4(tail("onorm", P)), ALU.mult))
                    of = oy[:, m, :, :].rearrange("p a b -> p (a b)")
                    return tt(of, of, zz[:, m, :], ALU.mult)
                dve_step(gate_o)
            transposes([(lambda m, i=i: oy[:, m, i, :], yaT[:, i, :], P, None, None) for i in range(4)])

            get = Carve(arena, raw_at)
            gg = get(TT, 2 * D)
            merged = get(TT, D)
            grow = get(2, D)
            cv2 = get(KD, S)
            rows_product(lambda k, m: uT[:, k, S + m * P:S + (m + 1) * P], KD, range(TT), [512] * 4,
                         lambda m, s, h0, n, b: read_out(b, fn_act=lambda: nc.scalar.activation(
                             gg[:, m, 512 * s:512 * s + n], bank[b][:, 0:n], ACT_F.Sigmoid)))

            def gated2(which):
                def read(m, s, h0, n, b):
                    def fn():
                        g = gg[:, m, which * D + h0:which * D + h0 + n]
                        if which == 0:
                            return tt(merged[:, m, h0:h0 + n], bank[b][:, 0:n], g, ALU.mult)
                        link(tt(g, bank[b][:, 0:n], g, ALU.mult))
                        return tt(merged[:, m, h0:h0 + n], merged[:, m, h0:h0 + n], g, ALU.add)
                    read_out(b, fn_dve=fn)
                return read

            if DVE:
                settle(DVE)
            for which, yt in ((0, yaT), (1, ybT)):
                rows_product(lambda k, m: yt[:, k, m * P:(m + 1) * P], 4, range(TT), [1024], gated2(which))
            dg = get(KD, P)
            for j, at in ((0, 16), (1, 40)):
                dve_step(lambda: tt(dg, ident.unsqueeze(1).to_broadcast([P, KD, P]),
                                    mod[:, at:at + KD, 0:1].to_broadcast([P, KD, P]), ALU.mult))
                for h in range(2):
                    pe_step(h, lambda bk: mm(bk[:, :], k2c("ones"), dg[:, 4 * h:4 * h + 4, :].rearrange("p a b -> p (a b)"),
                                             start=True, stop=True))
                    dve_step(lambda: nc.vector.tensor_copy(grow[:, j, 512 * h:512 * h + 512], bank[h][:, :]))
            transposes([(lambda m, k=k: merged[:, m, k * P:(k + 1) * P], cv2[:, k, :], P, None, None) for k in range(KD)])
            tmp = dg.rearrange("p a b -> p (a b)")

            def add_gated(j, m, at, n, src):
                g = grow[:, j, at:at + n]
                link(tt(tmp[:, 0:n], src, g, ALU.mult))
                return tt(x[:, m, at:at + n], x[:, m, at:at + n], tmp[:, 0:n], ALU.add)

            def link_first(fn):
                if DVE:
                    DVE.wait_ge(dve_done, c.dve)
                return fn()

            rows_product(lambda k, m: cv2[:, k, m * P:(m + 1) * P], KD, range(TT), [512, 512],
                         lambda m, s, h0, n, b: read_out(b, fn_dve=lambda: link_first(
                             lambda: add_gated(0, m, 512 * s, n, bank[b][:, 0:n]))))

            tT, xn = cv2, merged
            norm_rows(x[:, :, :], xn, TT)
            set_gain(col("ffn2", KD), 32)
            transposes([(lambda m, k=k: xn[:, m, k * P:(k + 1) * P], tT[:, k, :], P, gain[:, k, 0:1],
                         mod[:, 24 + k, 0:1]) for k in range(KD)])
            lgt = get(TT, 36)
            rows_product(lambda k, m: tT[:, k, m * P:(m + 1) * P], KD, range(TT), [36],
                         lambda m, s, h0, n, b: read_out(b, fn_dve=lambda: tt(
                             lgt[:, m, :], bank[b][:, 0:36], tail("rb", 36), ALU.add)))
            comb = get(TT, N_EXP)
            q = Carve(arena, get.at)
            get.at += 160
            one, cand, ing, oh1, oh2, we = q(8), q(8), q(8), q(8), q(8), q(8)
            sc1, sel4 = q(8), q(4, 8)

            def first_max(dst, src, n, best):
                link(nc.vector.tensor_reduce(best, src, AX, ALU.max))
                link(nc.vector.tensor_scalar(cand[:, 0:n], src, best, None, ALU.is_equal))
                link(nc.vector.scalar_tensor_tensor(cand[:, 0:n], cand[:, 0:n], -99.0, k2c("index", n), ALU.mult, ALU.add))
                link(nc.vector.tensor_reduce(sc1[:, 7:8], cand[:, 0:n], AX, ALU.min))
                link(nc.vector.tensor_scalar(dst, cand[:, 0:n], sc1[:, 7:8], None, ALU.is_equal))

            for m in range(TT):
                grp = lgt[:, m, 0:4]

                def route():
                    first_max(one[:, 0:4], grp, 4, sc1[:, 0:1])
                    exq = lgt[:, m, 4:36].rearrange("p (g e) -> p g e", g=4)
                    link(tt(sel4, exq, one[:, 0:4].unsqueeze(2).to_broadcast([P, 4, 8]), ALU.mult))
                    link(nc.vector.tensor_reduce(ing, sel4.rearrange("p g e -> p e g"), AX, ALU.add))
                    first_max(oh1, ing, 8, sc1[:, 1:2])
                    link(nc.vector.scalar_tensor_tensor(ing, oh1, HIDDEN, ing, ALU.mult, ALU.add))
                    first_max(oh2, ing, 8, sc1[:, 2:3])
                    link(nc.vector.tensor_scalar(grp, grp, sc1[:, 0:1], None, ALU.subtract))
                    return tt(sc1[:, 2:3], sc1[:, 2:3], sc1[:, 1:2], ALU.subtract)
                dve_step(route)

                def route_exp():
                    nc.scalar.activation(grp, grp, ACT_F.Exp, accum_out=sc1[:, 3:4])
                    return nc.scalar.activation(sc1[:, 2:3], sc1[:, 2:3], ACT_F.Exp)
                act_step(route_exp)

                def weights():
                    link(nc.vector.tensor_scalar(sc1[:, 4:5], sc1[:, 2:3], 1.0, None, ALU.add))
                    link(tt(sc1[:, 4:5], sc1[:, 4:5], sc1[:, 3:4], ALU.mult))
                    link(nc.vector.reciprocal(sc1[:, 4:5], sc1[:, 4:5]))
                    link(tt(sc1[:, 5:6], sc1[:, 4:5], sc1[:, 2:3], ALU.mult))
                    link(nc.vector.tensor_scalar(we, oh1, sc1[:, 4:5], None, ALU.mult))
                    link(nc.vector.scalar_tensor_tensor(we, oh2, sc1[:, 5:6], we, ALU.mult, ALU.add))
                    return tt(comb[:, m, :].rearrange("p (g e) -> p g e", g=4), we.unsqueeze(1).to_broadcast([P, 4, 8]),
                              one[:, 0:4].unsqueeze(2).to_broadcast([P, 4, 8]), ALU.mult)
                dve_step(weights)
            spread = Carve(arena, keep + ntail)(N_EXP, S)
            assert keep + ntail + N_EXP * S <= raw_at + TT * 2 * D, (keep, raw_at)
            combT = get(1, S)
            transposes([(lambda m: comb[:, m, :], combT[0:N_EXP, 0, :], N_EXP, None, None)])
            if PE:
                settle(PE)
            for e in range(0, N_EXP, 2):
                b = turn()
                take(b)
                if PE:
                    for j in range(2):
                        last = mm(bank[b][:, j * S:(j + 1) * S], ident[0:N_EXP, e + j:e + j + 1].to_broadcast([N_EXP, P]),
                                  combT[0:N_EXP, 0, :], start=True, stop=True)
                    last.then_inc(pe_done, 1)
                c.pe += 1
                copy_out(b, spread[:, e:e + 2, :], bank[b][:, :].rearrange("p (a b) -> p a b", a=2))

            hb = [get(2, 2, S) for _ in range(2)]
            if PE:
                settle(PE)
            if ACT:
                settle(ACT)
            if DVE:
                settle(DVE)
            for b in range(4, 8):
                take(b)
            ready, freed = {}, {}
            for e in range(N_EXP):
                w = open_slab()
                for j in range(2):
                    b = 2 * (e % 2) + j
                    take(b)
                    if PE:
                        for t in range(2):
                            for k in range(KD):
                                last = mm(bank[b][:, t * S:(t + 1) * S], w[:, ((2 * j + t) * KD + k) * P:((2 * j + t) * KD + k + 1) * P],
                                          tT[:, k, :], start=(k == 0), stop=(k == KD - 1))
                        last.then_inc(pe_done, 1)
                    c.pe += 1
                    if j == 0:
                        gate_ready = c.pe
                close_slab()
                h = hb[e % 2]
                bg, bu = 2 * (e % 2), 2 * (e % 2) + 1
                if ACT:
                    ACT.wait_ge(pe_done, gate_ready)
                    if e >= 2:
                        ACT.wait_ge(pe_done, freed[e - 2])
                    nc.scalar.activation(h[:, 0, :, :], bank[bg][:, :].rearrange("p (a b) -> p a b", a=2), ACT_F.Silu)\
                        .then_inc(act_done, 1)
                c.act += 1
                bank_free[bg] = ("act", c.act)
                if DVE:
                    DVE.wait_ge(act_done, c.act)
                    DVE.wait_ge(pe_done, c.pe)
                    link(tt(h[:, 1, :, :], bank[bu][:, :].rearrange("p (a b) -> p a b", a=2), h[:, 0, :, :], ALU.mult))
                    tt(h[:, 1, :, :], h[:, 1, :, :], spread[:, e, :].unsqueeze(1).to_broadcast([P, 2, S]), ALU.mult)\
                        .then_inc(dve_done, 1)
                c.dve += 1
                bank_free[bu] = ("dve", c.dve)
                ready[e] = c.dve
                if e % 2 == 1:
                    w = open_slab()
                    for j in range(2):
                        if PE:
                            PE.wait_ge(dve_done, ready[e - 1 + j])
                            for m in range(TT):
                                for half_ in range(2):
                                    for t in range(2):
                                        last = mm(bank[4 + 2 * m + half_][:, :], hb[j][:, 1, t, m * P:(m + 1) * P],
                                                  w[:, (2 * j + t) * D + half_ * 512:(2 * j + t) * D + half_ * 512 + 512],
                                                  start=(e == 1 and j == 0 and t == 0), stop=(e == N_EXP - 1 and j == 1 and t == 1))
                            last.then_inc(pe_done, 1)
                        c.pe += 1
                        freed[e - 1 + j] = c.pe
                    close_slab()
            for b in range(4, 8):
                m, h = divmod(b - 4, 2)
                read_out(b, fn_dve=lambda: link_first(lambda: add_gated(1, m, 512 * h, 512, bank[b][:, :])))
            norm_rows(x[:, :, :], xn, TT)
            for m in range(TT):
                dve_step(lambda: tt(xn[:, m, :], xn[:, m, :], tail("fin", D), ALU.mult))
            if SP:
                settle(SP)
                SP.dma_start(out.rearrange("b (m p) d -> p (b m) d", p=P), xn).then_inc(stored, 16)
                SP.wait_ge(stored, 16)

        block = ctx.enter_context(nc.Block())

        @block.sync
        def _(sp):
            program(SP=sp)

        @block.gpsimd
        def _(pool):
            program(POOL=pool)

        @block.scalar
        def _(act):
            program(ACT=act)

        @block.tensor
        def _(pe):
            program(PE=pe)

        @block.vector
        def _(dve):
            program(DVE=dve)


def pack(i):
    def blocks(w, n0, n1):
        k = w.shape[0] // P
        return w.reshape(k, P, w.shape[1])[:, :, n0:n1].transpose(1, 0, 2).reshape(P, -1)

    def tiles(w, ts):
        return [blocks(w, P * t, P * t + P) for t in ts]

    st = []
    for l in range(DEPTH):
        w = i["w_in"][l]
        st += [blocks(w, n, min(n + 512, IN1)) for n in range(0, IN1, 512)]
        st += tiles(i["ada_w_2"][0], range(24 * l, 24 * l + 8))
        st += [blocks(i["b_w_uq"][l], 0, 768), blocks(i["b_w_ukv"][l], 0, 1024)]
        st += tiles(i["ada_w_2"][0], range(24 * l + 8, 24 * l + 24))
        st += [blocks(i["w_proj_a"][l], 0, D), blocks(i["w_proj_b"][l], 0, D)]
        st += [blocks(i["w_out"][l], 0, 512), blocks(i["w_out"][l], 512, 1024)]
        for t in range(FT):
            st += tiles(i["w_up"][l], (t, FT + t))
        st.append(blocks(i["w_down"][l], 0, D))
    w = i["w_in_2"][0]
    ga, gb = 2064, 2064 + B_COLS
    st += [blocks(w, ga + n, ga + min(n + 512, B_COLS)) for n in range(0, B_COLS, 512)]
    st += tiles(w, range(12))
    st += [blocks(w, 1536, 2048), blocks(w, 2048, 2064)]
    st += [blocks(w, gb + 512 * n, gb + 512 * n + 512) for n in range(4)]
    st += [blocks(i["w_o_a_2"][0], 0, D), blocks(i["w_o_b_2"][0], 0, D)]
    st += [blocks(i["w_out_2"][0], 0, 512), blocks(i["w_out_2"][0], 512, 1024)]
    st += [np.concatenate([blocks(i["router_grp_2"][0], 0, 4).reshape(P, KD, 4),
                           blocks(i["router_exp_2"][0], 0, 32).reshape(P, KD, 32)], 2).reshape(P, -1)]
    wg = i["moe_w_gate_2"][0].reshape(N_EXP, D, 256)
    wu = i["moe_w_up_2"][0].reshape(N_EXP, D, 256)
    wd = i["moe_w_down_2"][0].reshape(N_EXP, 256, D)
    for e in range(0, N_EXP, 2):
        for j in range(2):
            st += tiles(wg[e + j], range(2)) + tiles(wu[e + j], range(2))
        st += [blocks(wd[e], 0, D), blocks(wd[e + 1], 0, D)]
    stream = np.concatenate(st, 1)
    assert stream.shape[1] == sum(slab_sizes()), (stream.shape, sum(slab_sizes()))

    def column(v):
        return v.reshape(-1, P).T

    cs = []
    for l in range(DEPTH):
        short = lambda v: np.concatenate([v, np.zeros(P - QK_B, v.dtype)]).reshape(P, 1)
        cs += [column(i["norm_mix"][l]), column(i["norm_ffn"][l]),
               np.concatenate([i["a_q_norm"][l]] * 2).reshape(P, 1), np.concatenate([i["a_k_norm"][l]] * 2).reshape(P, 1),
               column(i["b_cq_norm"][l]), column(i["b_ckv_norm"][l]), short(i["b_q_norm"][l]), short(i["b_k_norm"][l])]
        cs += [column(i["conv_w"][l][r]) for r in range(3)] + [column(i["conv_b"][l])]
    cs += [column(i["ada_b_2"][0]), column(i["c_2"][0]), column(i["c_ctx_2"]), column(i["norm_mix_g_2"][0]),
           column(i["norm_ffn_g_2"][0])] + [column(i["gdn_conv_2"][0][r]) for r in range(5)]
    cols = np.concatenate(cs, 1)
    assert cols.shape[1] == COL["all"]
    rows = np.concatenate([i["b_gate"].reshape(-1)] + [i[n + "_2"][0].reshape(-1) for n in (
        "rwkv_mu", "rwkv_w0", "rwkv_a0", "rwkv_k_k", "rwkv_k_a", "rwkv_r_k", "rwkv_lnx_g", "rwkv_lnx_b",
        "gdn_a_log", "gdn_dt_bias", "gdn_onorm_g", "router_grp_b", "router_exp_b")] + [i["final_norm_g_2"].reshape(-1)])[None]
    lora = np.concatenate([i["rwkv_w2_2"][0].reshape(P, 512), i["rwkv_a2_2"][0].reshape(P, 512),
                           i["rwkv_g2_2"][0].reshape(P, 512)], 1)
    return stream, cols, rows, lora


def kernel(**inputs):
    import concourse.bacc as bacc
    from concourse.bass_utils import run_bass_kernel_spmd

    i = {n: np.asarray(a) for n, a in inputs.items()}
    stream, cols, rows, lora = pack(i)
    k1, k2 = constants()
    arrays = {"stream": stream, "columns_in": cols, "rows_in": rows, "constants_1": k1, "constants_2": k2,
              "lora_in": lora, "x_in": i["x"], "ctx_in": i["ctx_2"], "rel_bias_in": i["rel_bias"]}
    arrays = {n: np.ascontiguousarray(a) for n, a in arrays.items()}
    nc = bacc.Bacc("TRN2", target_bir_lowering=False, num_devices=1)
    ap = {n: nc.dram_tensor(n, a.shape, F32, kind="ExternalInput").ap() for n, a in arrays.items()}
    out = nc.dram_tensor("out", (1, S, D), F32, kind="ExternalOutput").ap()
    build(nc, ap["stream"], ap["columns_in"], ap["rows_in"], ap["constants_1"], ap["constants_2"], ap["lora_in"],
          ap["x_in"], ap["ctx_in"], ap["rel_bias_in"], out)
    r = run_bass_kernel_spmd(nc, [arrays], core_ids=[0])
    return r.results[0]["out"]
```
